# Optimizing a Trainium2 kernel written in Bass

```python
import jax, jax.numpy as jnp
from jax import lax
import numpy as np

D_MODEL = 1024
BATCH = 1
SEQ = 512
DEPTH = 1

HEAD_DIM = 64
MOBA_HEADS = 8
MOBA_BLOCK = 256
MOBA_TOPK = 3
SWA_Q_HEADS = 8
SWA_KV_HEADS = 2
SWA_WINDOW = 128
N_REL_BUCKETS = 32
REL_MAX_DISTANCE = 2048
D_FF = 4 * D_MODEL
Q_CHUNK = 128
NORM_EPS = 1e-6

MOBA_WIDTH = MOBA_HEADS * HEAD_DIM
SWA_Q_WIDTH = SWA_Q_HEADS * HEAD_DIM
SWA_KV_WIDTH = SWA_KV_HEADS * HEAD_DIM
N_ATTN_HEADS = MOBA_HEADS + SWA_Q_HEADS
IN_WIDTH = 3 * MOBA_WIDTH + SWA_Q_WIDTH + 2 * SWA_KV_WIDTH + 2 * D_MODEL

kernel_name = "hybrid_moba_swa_gated_block"

def rms_norm(x, g):
    xf = x.astype(jnp.float32)
    y = xf * lax.rsqrt(jnp.mean(xf * xf, axis=-1, keepdims=True) + NORM_EPS)
    return (y * g.astype(jnp.float32)).astype(x.dtype)

def rel_bucket(dist):
    n = jnp.maximum(dist, 0)
    exact = N_REL_BUCKETS // 2
    nf = jnp.maximum(n, 1).astype(jnp.float32)
    large = exact + (jnp.log(nf / exact) / np.float32(np.log(REL_MAX_DISTANCE / exact))
                     * (N_REL_BUCKETS - exact)).astype(jnp.int32)
    large = jnp.minimum(large, N_REL_BUCKETS - 1)
    return jnp.where(n < exact, n, large)

def moba_attention(q, k, v, bias_table):
    B, H, S, hd = q.shape
    nb = -(-S // MOBA_BLOCK)
    pad = nb * MOBA_BLOCK - S
    kp = jnp.pad(k, ((0, 0), (0, 0), (0, pad), (0, 0)))
    vp = jnp.pad(v, ((0, 0), (0, 0), (0, pad), (0, 0)))
    kb = kp.reshape(B, H, nb, MOBA_BLOCK, hd)
    vb = vp.reshape(B, H, nb, MOBA_BLOCK, hd)
    kmean = jnp.mean(kb.astype(jnp.float32), axis=3)
    gate = jnp.einsum('bhsd,bhnd->bhsn', q.astype(jnp.float32), kmean)
    qblk = jnp.arange(S) // MOBA_BLOCK
    past = jnp.arange(nb)[None, :] < qblk[:, None]
    gate = jnp.where(past[None, None], gate, -jnp.inf)
    n_sel = min(MOBA_TOPK, nb)
    _, sel = lax.top_k(gate, n_sel)
    sel_valid = sel < qblk[None, None, :, None]
    scale = HEAD_DIM ** -0.5
    n_chunks = S // Q_CHUNK
    q_c = q.reshape(B, H, n_chunks, Q_CHUNK, hd).transpose(2, 0, 1, 3, 4)
    sel_c = sel.reshape(B, H, n_chunks, Q_CHUNK, n_sel).transpose(2, 0, 1, 3, 4)
    val_c = sel_valid.reshape(B, H, n_chunks, Q_CHUNK, n_sel).transpose(2, 0, 1, 3, 4)
    b_ix = jnp.arange(B)[:, None, None, None]
    h_ix = jnp.arange(H)[None, :, None, None]
    h5 = jnp.arange(H)[None, :, None, None, None]
    offs = jnp.arange(MOBA_BLOCK)
    bias_t = bias_table.T.astype(jnp.float32)
    n_past = n_sel * MOBA_BLOCK

    def chunk(args):
        c, qc, sc, vc = args
        qpos = c * Q_CHUNK + jnp.arange(Q_CHUNK)
        kg = kb[b_ix, h_ix, sc]
        vg = vb[b_ix, h_ix, sc]
        lp = jnp.einsum('bhqd,bhqnkd->bhqnk', qc, kg).astype(jnp.float32) * scale
        kpos_p = sc[..., None] * MOBA_BLOCK + offs
        lp = lp + bias_t[h5, rel_bucket(qpos[None, None, :, None, None] - kpos_p)]
        lp = jnp.where(vc[..., None], lp, -jnp.inf)
        ob = (c * Q_CHUNK) // MOBA_BLOCK
        ko = lax.dynamic_index_in_dim(kb, ob, axis=2, keepdims=False)
        vo = lax.dynamic_index_in_dim(vb, ob, axis=2, keepdims=False)
        lo = jnp.einsum('bhqd,bhkd->bhqk', qc, ko).astype(jnp.float32) * scale
        d_o = qpos[:, None] - (ob * MOBA_BLOCK + offs)[None, :]
        lo = lo + bias_t[:, rel_bucket(d_o)][None]
        lo = jnp.where((d_o >= 0)[None, None], lo, -jnp.inf)
        logits = jnp.concatenate([lp.reshape(B, H, Q_CHUNK, n_past), lo], axis=-1)
        p = jax.nn.softmax(logits, axis=-1)
        out = (jnp.einsum('bhqk,bhqkd->bhqd', p[..., :n_past].astype(vg.dtype),
                          vg.reshape(B, H, Q_CHUNK, n_past, hd))
               + jnp.einsum('bhqk,bhkd->bhqd', p[..., n_past:].astype(vo.dtype), vo))
        return out.astype(q.dtype)

    outs = lax.map(chunk, (jnp.arange(n_chunks), q_c, sel_c, val_c))
    return outs.transpose(1, 2, 0, 3, 4).reshape(B, H, S, hd)

def swa_attention(q, k, v, sinks, bias_table):
    B, HQ, S, hd = q.shape
    HKV = k.shape[1]
    G = HQ // HKV
    W = SWA_WINDOW
    nb = S // W
    qb = q.reshape(B, HKV, G, nb, W, hd)
    kb = k.reshape(B, HKV, nb, W, hd)
    vb = v.reshape(B, HKV, nb, W, hd)
    zpad = ((0, 0), (0, 0), (1, 0), (0, 0), (0, 0))
    kband = jnp.concatenate([jnp.pad(kb, zpad)[:, :, :-1], kb], axis=3)
    vband = jnp.concatenate([jnp.pad(vb, zpad)[:, :, :-1], vb], axis=3)
    scale = HEAD_DIM ** -0.5
    logits = jnp.einsum('bkgnqd,bkncd->bkgnqc', qb, kband).astype(jnp.float32) * scale
    kj = jnp.arange(2 * W) - W
    dist = jnp.arange(W)[:, None] - kj[None, :]
    bias = bias_table.T.astype(jnp.float32)[:, rel_bucket(dist)].reshape(HKV, G, 1, W, 2 * W)
    in_win = (dist >= 0) & (dist < W)
    real = (jnp.arange(nb)[:, None] * W + kj[None, :]) >= 0
    mask = in_win[None] & real[:, None, :]
    logits = jnp.where(mask, logits + bias, -jnp.inf)
    sink = jnp.broadcast_to(sinks.astype(jnp.float32).reshape(1, HKV, G, 1, 1, 1),
                            logits.shape[:-1] + (1,))
    p = jax.nn.softmax(jnp.concatenate([logits, sink], axis=-1), axis=-1)[..., :-1]
    out = jnp.einsum('bkgnqc,bkncd->bkgnqd', p.astype(vband.dtype), vband)
    return out.reshape(B, HQ, S, hd).astype(q.dtype)

def _heads(t, n):
    B, S, _ = t.shape
    return t.reshape(B, S, n, HEAD_DIM).transpose(0, 2, 1, 3)

def _merge_heads(t):
    B, H, S, hd = t.shape
    return t.transpose(0, 2, 1, 3).reshape(B, S, H * hd)

def setup_inputs(seed: int = 0) -> dict:
    key = jax.random.key(seed)
    ks = jax.random.split(key, 20)
    f32 = jnp.float32
    nrm = lambda k, shape, s: jax.random.normal(k, shape, f32) * s
    return {
        "x": nrm(ks[0], (BATCH, SEQ, D_MODEL), 1.0),
        "rel_bias": nrm(ks[1], (N_REL_BUCKETS, N_ATTN_HEADS), 0.5),
        "g_mix": 1.0 + nrm(ks[2], (DEPTH, D_MODEL), 0.02),
        "w_in": nrm(ks[3], (DEPTH, D_MODEL, IN_WIDTH), D_MODEL ** -0.5),
        "b_gate": nrm(ks[4], (DEPTH, 2 * D_MODEL), 0.02),
        "q_norm_a": 1.0 + nrm(ks[5], (DEPTH, HEAD_DIM), 0.02),
        "k_norm_a": 1.0 + nrm(ks[6], (DEPTH, HEAD_DIM), 0.02),
        "q_norm_b": 1.0 + nrm(ks[7], (DEPTH, HEAD_DIM), 0.02),
        "k_norm_b": 1.0 + nrm(ks[8], (DEPTH, HEAD_DIM), 0.02),
        "sinks": nrm(ks[9], (DEPTH, SWA_Q_HEADS), 0.5),
        "w_branch_a": nrm(ks[10], (DEPTH, MOBA_WIDTH, D_MODEL), MOBA_WIDTH ** -0.5),
        "w_branch_b": nrm(ks[11], (DEPTH, SWA_Q_WIDTH, D_MODEL), SWA_Q_WIDTH ** -0.5),
        "w_out": nrm(ks[12], (DEPTH, D_MODEL, D_MODEL), D_MODEL ** -0.5),
        "g_ffn": 1.0 + nrm(ks[13], (DEPTH, D_MODEL), 0.02),
        "w_ff1": nrm(ks[14], (DEPTH, D_MODEL, D_FF), D_MODEL ** -0.5),
        "w_ff2": nrm(ks[15], (DEPTH, D_FF, D_MODEL), D_FF ** -0.5),
    }

def reference(x, rel_bias, g_mix, w_in, b_gate, q_norm_a, k_norm_a, q_norm_b, k_norm_b,
              sinks, w_branch_a, w_branch_b, w_out, g_ffn, w_ff1, w_ff2):
    bias_a = rel_bias[:, :MOBA_HEADS]
    bias_b = rel_bias[:, MOBA_HEADS:]
    splits = np.cumsum([MOBA_WIDTH, MOBA_WIDTH, MOBA_WIDTH, SWA_Q_WIDTH,
                        SWA_KV_WIDTH, SWA_KV_WIDTH, D_MODEL]).tolist()
    for l in range(DEPTH):
        h = rms_norm(x, g_mix[l])
        proj = h @ w_in[l]
        qa, ka, va, qb, kb, vb, ga, gb = jnp.split(proj, splits, axis=-1)
        qa = rms_norm(_heads(qa, MOBA_HEADS), q_norm_a[l])
        ka = rms_norm(_heads(ka, MOBA_HEADS), k_norm_a[l])
        va = _heads(va, MOBA_HEADS)
        qb = rms_norm(_heads(qb, SWA_Q_HEADS), q_norm_b[l])
        kb = rms_norm(_heads(kb, SWA_KV_HEADS), k_norm_b[l])
        vb = _heads(vb, SWA_KV_HEADS)
        ya = _merge_heads(moba_attention(qa, ka, va, bias_a))
        yb = _merge_heads(swa_attention(qb, kb, vb, sinks[l], bias_b))
        gate_a = jax.nn.sigmoid((ga + b_gate[l, :D_MODEL]).astype(jnp.float32)).astype(x.dtype)
        gate_b = jax.nn.sigmoid((gb + b_gate[l, D_MODEL:]).astype(jnp.float32)).astype(x.dtype)
        merged = gate_a * (ya @ w_branch_a[l]) + gate_b * (yb @ w_branch_b[l])
        x = x + merged @ w_out[l]
        h2 = rms_norm(x, g_ffn[l])
        x = x + jnp.square(jax.nn.relu(h2 @ w_ff1[l])) @ w_ff2[l]
    return x


_drawn_inputs = setup_inputs


def setup_inputs(seed=0):
    import zlib

    import numpy as np

    out = dict(_drawn_inputs(seed))
    spreads = {}
    factors = {'g_mix': 8.0,
     'b_gate': 8.0,
     'q_norm_a': 8.0,
     'k_norm_a': 8.0,
     'q_norm_b': 8.0,
     'k_norm_b': 8.0,
     'sinks': 29.841,
     'g_ffn': 8.669}
    for name, (base, spread) in spreads.items():
        noise = np.random.default_rng([zlib.crc32(name.encode()), seed]).standard_normal(out[name].shape)
        drawn = base * np.exp(spread * noise) if base else spread * noise
        out[name] = __import__('jax').numpy.asarray(drawn.astype(out[name].dtype))
    for name, factor in factors.items():
        out[name] = (out[name] * factor).astype(out[name].dtype)
    return out
```

```python
import numpy as np
import concourse.bass as bass
from concourse import mybir
from contextlib import ExitStack

D, S, HD, DFF = 1024, 512, 64, 4096
P = 128
KT = D // P
QT = S // P
NBUCKET, MAXDIST, WINDOW = 32, 2048, 128
EPS = 1e-6
MASK = -1e30
NH = 16

KV_B, V_B = 0, 5
N_QKV, N_GATE, N_BRANCH, N_OUT = 18, 16, 8, 8
G_GATE = N_QKV
G_BRANCH = G_GATE + N_GATE
G_OUT = G_BRANCH + N_BRANCH
G_FF = G_OUT + N_OUT
CHUNKS = 4
PER_CHUNK = 16
N_SLABS = G_FF + CHUNKS * PER_CHUNK
RAW, WS = 4, 2

QKV_KIND = ["k", "q", "q", "q", "q", "v"] + ["k", "q"] * 4 + ["v"] * 4
QKV_TILE = [0, 1, 2, 3, 4, 0] + [5, 9, 6, 10, 7, 11, 8, 12] + [1, 2, 3, 4]
Y_B, Y_A = 1, 9
C_MIX, C_FFN, C_BGATE, C_NORM, C_SINK, N_PAR = 0, 8, 16, 32, 36, 44
T_A, T_B, N_TAB = 0, 640, 1024
P_BASE = [0, 128, 384, 768]


def norm_column(slab):
    return C_NORM + (0 if slab < V_B else 2) + (QKV_KIND[slab] == "q")


def build(nc, x_t, slabs, params, table, onehot, tab_dram, out):
    F32, R = mybir.dt.float32, mybir.dt.float32r
    ALU, ACT = mybir.AluOpType, mybir.ActivationFunctionType
    ctx = ExitStack()
    with ctx:
        def sb(name, shape, dt):
            return ctx.enter_context(nc.sbuf_tensor(name, shape, dt))

        def sem(name):
            return ctx.enter_context(nc.semaphore(name))

        w_raw = sb("w_raw", [P, RAW, D], F32)
        w_hi, w_lo = sb("w_hi", [P, WS, D], R), sb("w_lo", [P, WS, D], R)
        x_hi, x_lo = sb("x_hi", [P, KT, S], R), sb("x_lo", [P, KT, S], R)
        qk_hi, qk_lo = sb("qk_hi", [P, 13, S], R), sb("qk_lo", [P, 13, S], R)
        v_hi, v_lo = sb("v_hi", [P, 5, QT, 3, HD], R), sb("v_lo", [P, 5, QT, 3, HD], R)
        store = sb("store", [P, 16, S], F32)
        pt_hi, pt_lo = sb("pt_hi", [P, QT, S], R), sb("pt_lo", [P, QT, S], R)
        probs = sb("probs", [P, 1280], F32)
        bias_m = sb("bias_m", [P, 2, S], F32)
        r_all = sb("r_all", [P, S], F32)
        ident = sb("ident", [P, P], F32)
        ones = sb("ones", [P, P], F32)
        head_ones = sb("head_ones", [P, P], F32)
        par = sb("par", [P, N_PAR], F32)
        top = sb("top", [P, QT], F32)
        neg = sb("neg", [P, QT], F32)
        den = sb("den", [P, QT], F32)
        sink_e = sb("sink_e", [P, QT], F32)
        rec = sb("rec", [P, QT], F32)
        bank = [ctx.enter_context(nc.psum_tensor(f"bank{i}", [P, 512], F32)) for i in range(8)]

        xsq = [store[:, 8, :], store[:, 9, :]]
        tab = store[0:NH, 10:12, :].rearrange("p a n -> p (a n)")
        x_sum = store[:, 12, :]
        eps_r = store[:, 12, :]
        pre = store[:, 13, :]
        sq = store[:, 14, :]
        inv = store[:, 15, :]
        hot = probs[0:NBUCKET + 1, 0:N_TAB]
        tabw = probs[0:NBUCKET + 1, N_TAB:N_TAB + NH]
        tmp_a, tmp_b = probs[:, 0:S], probs[:, S:2 * S]

        arrived = [sem(f"slab_arrived{i}") for i in range(RAW)]
        x_arrived = [sem(f"x_arrived{i}") for i in range(KT)]
        par_arrived = sem("par_arrived")
        tab_arrived = sem("tab_arrived")
        tab_stored = sem("tab_stored")
        bias_arrived = [sem("bias_arrived0"), sem("bias_arrived1")]
        out_stored = sem("out_stored")
        const_ready, ident_ready = sem("const_ready"), sem("ident_ready")
        par_ready = sem("par_ready")
        w_hi_ready, w_lo_ready = sem("w_hi_ready"), sem("w_lo_ready")
        slab_done = sem("slab_done")
        acc_read = sem("acc_read")
        x_hi_ready, x_lo_ready = sem("x_hi_ready"), sem("x_lo_ready")
        xsq_ready, xsum_ready = sem("xsq_ready"), sem("xsum_ready")
        ms_done, ms_ready, r_sqrt, r_ready = sem("ms_done"), sem("ms_ready"), sem("r_sqrt"), sem("r_ready")
        tab_done, tab_copied = sem("tab_done"), sem("tab_copied")
        sq_ready, ss_done, ss_read = sem("sq_ready"), sem("ss_done"), sem("ss_read")
        sqrt_ready, inv_ready = sem("sqrt_ready"), sem("inv_ready")
        qk_hi_ready, qk_lo_ready = sem("qk_hi_ready"), sem("qk_lo_ready")
        vt_done, v_hi_ready, v_lo_ready = sem("vt_done"), sem("v_hi_ready"), sem("v_lo_ready")
        scores_done, max_ready, neg_ready = sem("scores_done"), sem("max_ready"), sem("neg_ready")
        exp_ready, sink_ready = sem("exp_ready"), sem("sink_ready")
        den_ready, rec_ready, probs_ready = sem("den_ready"), sem("rec_ready"), sem("probs_ready")
        pt_done, pt_hi_ready, pt_lo_ready = sem("pt_done"), sem("pt_hi_ready"), sem("pt_lo_ready")
        pv_done, y_hi_ready, y_lo_ready = sem("pv_done"), sem("y_hi_ready"), sem("y_lo_ready")
        gate_ready = sem("gate_ready")
        part_ready, m_ready = sem("part_ready"), sem("m_ready")
        m_hi_ready, m_lo_ready = sem("m_hi_ready"), sem("m_lo_ready")
        x2_arrived = [sem(f"x2_arrived{i}") for i in range(KT)]
        x1_hi_ready, x1_lo_ready = sem("x1_hi_ready"), sem("x1_lo_ready")
        x1sq_ready, x1sum_ready = sem("x1sq_ready"), sem("x1sum_ready")
        ms2_done, ms2_ready, r2_ready = sem("ms2_done"), sem("ms2_ready"), sem("r2_ready")
        relu_ready, u_hi_ready, u_lo_ready = sem("relu_ready"), sem("u_hi_ready"), sem("u_lo_ready")
        sum_ready, scaled_ready, out_ready = sem("sum_ready"), sem("scaled_ready"), sem("out_ready")

        def qk_count(slab):
            return sum(kind != "v" for kind in QKV_KIND[:slab])

        def v_count(slab):
            return sum(kind == "v" for kind in QKV_KIND[:slab])

        N_QK, N_V = qk_count(N_QKV), v_count(N_QKV)

        def key_tiles(i, qt):
            return QT - 1 - qt, min(2, qt + 1) if i < 8 else qt + 1

        def order(i, qt):
            return QT * i + (QT - 1 - qt)

        HALVES = [(3, 2), (1, 0)]

        block = ctx.enter_context(nc.Block())

        @block.sync
        def _(sp):
            def load_slab(g):
                if g >= RAW:
                    sp.wait_ge(w_lo_ready, g - RAW + 1)
                sp.dma_start(w_raw[:, g % RAW, :], slabs[g]).then_inc(arrived[g % RAW], 16)

            def load_bias(i):
                if i >= 2:
                    sp.wait_ge(max_ready, QT * (i - 1))
                else:
                    sp.wait_ge(tab_stored, 16)
                at, n = (T_B, 2 * P) if i < 8 else (T_A, S)
                src = bass.AP(tensor=tab_dram.tensor, offset=i * N_TAB + at, ap=[[1, P], [1, n]])
                sp.dma_start(bias_m[:, i % 2, 0:n], src).then_inc(bias_arrived[i % 2], 16)

            sp.dma_start(par[:, :], params).then_inc(par_arrived, 16)
            load_slab(0)
            for k in range(KT):
                sp.dma_start(store[:, k, :], x_t[k]).then_inc(x_arrived[k], 16)
                if k == 3:
                    load_slab(1)
            sp.dma_start(hot, onehot).then_inc(tab_arrived, 16)
            sp.dma_start(tabw[0:NBUCKET, :], table).then_inc(tab_arrived, 16)
            for g in range(2, G_FF):
                if g == 14:
                    sp.wait_ge(tab_copied, 2)
                    sp.dma_start(tab_dram, tab).then_inc(tab_stored, 16)
                if g == 16:
                    load_bias(0)
                    load_bias(1)
                if 2 <= g - 22 < NH:
                    load_bias(g - 22)
                if G_BRANCH + 6 <= g < G_OUT + 6:
                    n = g - G_BRANCH - 6
                    sp.wait_ge(acc_read, G_BRANCH + n + 1)
                    sp.dma_start(store[:, n, :], x_t[n]).then_inc(x2_arrived[n], 16)
                load_slab(g)
            with sp.Fori(0, CHUNKS) as c:
                for k in range(PER_CHUNK):
                    g = sp.snap(c * PER_CHUNK + (G_FF + k))
                    sp.wait_ge(w_lo_ready, c * PER_CHUNK + (G_FF + k - RAW + 1))
                    sp.dma_start(w_raw[:, (G_FF + k) % RAW, :],
                                 slabs[bass.ds(g, 1)].rearrange("a p n -> (a p) n")
                                 ).then_inc(arrived[(G_FF + k) % RAW], 16)
            for n in range(KT):
                sp.wait_ge(out_ready, n + 1)
                sp.dma_start(out[n], store[:, 8 + n, :]).then_inc(out_stored, 16)
            sp.wait_ge(out_stored, 16 * KT)

        @block.gpsimd
        def _(pool):
            pool.memset(ident[:, :], 0.0).then_inc(ident_ready, 1)
            pool.wait_ge(ident_ready, 1)
            pool.affine_select(out=ident[:, :], in_=ident[:, :], compare_op=ALU.not_equal, fill=1.0,
                               base=0, pattern=[[-1, P]], channel_multiplier=1).then_inc(ident_ready, 1)

            def split_lo(g, count):
                pool.wait_ge(w_hi_ready, count)
                pool.tensor_tensor(w_lo[:, g % WS, :], w_raw[:, g % RAW, :],
                                   w_hi[:, g % WS, :].bitcast(F32), ALU.subtract).then_inc(w_lo_ready, 1)

            for g in range(2):
                split_lo(g, g + 1)
            with pool.Fori(0, (N_SLABS - 2) // RAW) as c:
                for k in range(RAW):
                    split_lo(2 + k, c * RAW + (2 + k + 1))

        @block.scalar
        def _(act):
            def split_hi(g, c=None):
                at = 0 if c is None else c * PER_CHUNK
                act.wait_ge(arrived[g % RAW], 16 * (g // RAW + 1) + (0 if c is None else c * (16 * PER_CHUNK // RAW)))
                if g >= WS:
                    act.wait_ge(slab_done, at + (g - WS + 1))
                act.activation(w_hi[:, g % WS, :], w_raw[:, g % RAW, :], ACT.Copy).then_inc(w_hi_ready, 1)

            split_hi(0)
            act.wait_ge(par_arrived, 16)
            for k in range(KT):
                if k == 4:
                    split_hi(1)
                act.wait_ge(x_arrived[k], 16)
                act.activation(x_hi[:, k, :], store[:, k, :], ACT.Copy,
                               scale=par[:, C_MIX + k:C_MIX + k + 1]).then_inc(x_hi_ready, 1)
            for k in range(KT):
                if k >= 3:
                    act.wait_ge(xsum_ready, k - 2)
                act.activation(xsq[k % 2] if k else x_sum, store[:, k, :], ACT.Square).then_inc(xsq_ready, 1)

            def qkv_square(g):
                if QKV_KIND[g] != "v":
                    n = qk_count(g)
                    act.wait_ge(slab_done, g + 1)
                    if n:
                        act.wait_ge(ss_done, n)
                    act.activation(sq, bank[g % 3][:, :], ACT.Square).then_inc(sq_ready, 1)

            def qkv_hi(g):
                t = QKV_TILE[g]
                if QKV_KIND[g] != "v":
                    act.wait_ge(acc_read, g + 1)
                    act.activation(qk_hi[:, t, :], pre, ACT.Copy).then_inc(qk_hi_ready, 1)
                else:
                    act.wait_ge(vt_done, v_count(g) + 1)
                    if v_count(g) == 0:
                        act.wait_ge(const_ready, 4)
                    act.activation(v_hi[:, t, :, 0::2, :],
                                   bank[5][:, :].rearrange("p (t e d) -> p t e d", t=QT, e=2),
                                   ACT.Copy).then_inc(v_hi_ready, 1)

            def qkv_sqrt(g):
                if QKV_KIND[g] != "v":
                    act.wait_ge(ss_read, qk_count(g) + 1)
                    act.activation(inv, inv, ACT.Sqrt).then_inc(sqrt_ready, 1)

            for g in range(N_QKV):
                split_hi(g + 2)
                qkv_square(g)
                if g:
                    qkv_hi(g - 1)
                else:
                    act.wait_ge(ms_ready, 2)
                    act.activation(r_all[:, :], r_all[:, :], ACT.Sqrt).then_inc(r_sqrt, 1)
                qkv_sqrt(g)

            def exps(i, half):
                act.wait_ge(neg_ready, 2 * i + half + 1)
                for qt in HALVES[half]:
                    n = P * key_tiles(i, qt)[1]
                    s = probs[:, P_BASE[qt]:P_BASE[qt] + n]
                    act.activation(s, s, ACT.Exp, bias=neg[:, qt:qt + 1],
                                   accum_out=den[:, qt:qt + 1]).then_inc(exp_ready, 1)
                if i < 8:
                    a = HALVES[half][1]
                    act.activation(sink_e[:, a:a + 2], neg[:, a:a + 2], ACT.Exp,
                                   bias=par[:, C_SINK + i:C_SINK + i + 1]).then_inc(sink_ready, 1)

            def probs_t_hi(i, qt):
                n = order(i, qt)
                k0, nk = key_tiles(i, qt)
                act.wait_ge(pt_done, n + 1)
                act.activation(pt_hi[:, k0:k0 + nk, P * qt:P * qt + P],
                               bank[5 + n % 2][:, 0:P * nk].rearrange("p (k q) -> p k q", k=nk),
                               ACT.Copy).then_inc(pt_hi_ready, 1)

            exps(0, 0)
            exps(0, 1)
            qkv_hi(N_QKV - 1)
            for i in range(NH):
                probs_t_hi(i, 3)
                probs_t_hi(i, 2)
                if i + 1 < NH:
                    exps(i + 1, 0)
                probs_t_hi(i, 1)
                probs_t_hi(i, 0)
                if i + 1 < NH:
                    exps(i + 1, 1)
                split_hi(G_GATE + 2 + i)
                if i % 2:
                    act.wait_ge(pv_done, i + 1)
                    act.activation(qk_hi[:, (Y_B + i // 2) if i < 8 else (Y_A + i // 2 - 4), :],
                                   bank[7][:, :], ACT.Copy).then_inc(y_hi_ready, 1)

            def gate(n):
                for j in (n, 8 + n):
                    act.wait_ge(acc_read, G_GATE + j + 1)
                    act.activation(store[:, j, :], store[:, j, :], ACT.Sigmoid,
                                   bias=par[:, C_BGATE + j:C_BGATE + j + 1]).then_inc(gate_ready, 1)

            gate(0)
            for n in range(N_BRANCH):
                split_hi(G_BRANCH + n + 2)
                if n + 1 < N_BRANCH:
                    gate(n + 1)
                act.wait_ge(m_ready, n + 1)
                act.activation(x_hi[:, n, :], tmp_a, ACT.Copy).then_inc(m_hi_ready, 1)

            for n in range(N_OUT):
                act.wait_ge(acc_read, G_OUT + n + 1)
                act.activation(qk_hi[:, n, :], store[:, n, :], ACT.Copy,
                               scale=par[:, C_FFN + n:C_FFN + n + 1]).then_inc(x1_hi_ready, 1)
                split_hi(G_OUT + n + 2)
                if n >= 3:
                    act.wait_ge(x1sum_ready, n - 2)
                act.activation((tmp_a, tmp_b)[n % 2] if n else r_all[:, :], store[:, n, :],
                               ACT.Square).then_inc(x1sq_ready, 1)

            def up(j, c, last=False):
                g = G_FF + j
                at = c * PER_CHUNK
                act.wait_ge(slab_done, at + (g + 1))
                act.activation(tmp_a, bank[g % 2][:, :], ACT.Relu).then_inc(relu_ready, 1)
                if isinstance(c, int):
                    split_hi(g + 2 + c * PER_CHUNK)
                else:
                    split_hi(g + 2, c)
                act.wait_ge(acc_read, at + (g + 1))
                act.activation(x_hi[:, j, :], tmp_b, ACT.Copy).then_inc(u_hi_ready, 1)

            act.wait_ge(x1sum_ready, N_OUT - 1)
            with act.Fori(0, CHUNKS - 1) as c:
                for j in range(8):
                    up(j, c)
                for n in range(8):
                    split_hi(G_FF + 8 + n + 2, c)
            for j in range(8):
                up(j, CHUNKS - 1)
            for n in range(6):
                split_hi(N_SLABS - 8 + n + 2)

        @block.vector
        def _(dve):
            dve.memset(v_hi[:, :, :, 1, :].bitcast(F32), 0.0).then_inc(const_ready, 1)
            dve.memset(v_lo[:, :, :, 1, :].bitcast(F32), 0.0).then_inc(const_ready, 1)
            dve.memset(ones[:, :], 1.0 / D)
            for a in range(2):
                for b in range(2):
                    last = dve.memset(head_ones[HD * a:HD * (a + 1), HD * b:HD * (b + 1)],
                                      1.0 / HD if a == b else 0.0)
            last.then_inc(const_ready, 1)
            dve.memset(tabw[NBUCKET:NBUCKET + 1, :], MASK).then_inc(const_ready, 1)
            dve.wait_ge(par_arrived, 16)
            for a in (1, 3):
                col = par[:, C_NORM + a:C_NORM + a + 1]
                dve.tensor_scalar(col, col, HD ** -0.5, None, ALU.mult).then_inc(par_ready, 1)
            for k in range(KT):
                dve.wait_ge(x_hi_ready, k + 1)
                dve.scalar_tensor_tensor(out=x_lo[:, k, :], in0=store[:, k, :],
                                         scalar=par[:, C_MIX + k:C_MIX + k + 1],
                                         in1=x_hi[:, k, :].bitcast(F32), op0=ALU.mult,
                                         op1=ALU.subtract).then_inc(x_lo_ready, 1)
            for k in range(1, KT):
                dve.wait_ge(xsq_ready, k + 1)
                if k > 1:
                    dve.wait_ge(xsum_ready, k - 1)
                dve.tensor_tensor(x_sum, x_sum, xsq[k % 2], ALU.add).then_inc(xsum_ready, 1)
            dve.wait_ge(ms_done, 1)
            dve.tensor_scalar(r_all[:, :], bank[6][:, :], EPS, None, ALU.add).then_inc(ms_ready, 1)
            dve.wait_ge(ms_ready, 1)
            dve.tensor_scalar(eps_r, r_all[:, :], EPS, None, ALU.mult).then_inc(ms_ready, 1)
            dve.wait_ge(r_sqrt, 1)
            dve.reciprocal(r_all[:, :], r_all[:, :]).then_inc(r_ready, 1)

            def qkv_main(g):
                if QKV_KIND[g] != "v":
                    n = qk_count(g)
                    dve.wait_ge(ss_done, n + 1)
                    if n == 0:
                        dve.wait_ge(ms_ready, 2)
                    dve.tensor_tensor(inv, bank[3 + n % 2][:, :], eps_r, ALU.add).then_inc(ss_read, 1)
                    dve.wait_ge(sqrt_ready, n + 1)
                    dve.reciprocal(inv, inv).then_inc(inv_ready, 1)
                    dve.wait_ge(inv_ready, n + 1)
                    dve.wait_ge(par_ready, 2)
                    c = norm_column(g)
                    to = pre[:, ::-1] if QKV_KIND[g] == "k" else pre
                    dve.scalar_tensor_tensor(out=to, in0=bank[g % 3][:, :], scalar=par[:, c:c + 1],
                                             in1=inv, op0=ALU.mult, op1=ALU.mult).then_inc(acc_read, 1)
                else:
                    dve.wait_ge(slab_done, g + 1)
                    dve.wait_ge(r_ready, 1)
                    if QKV_KIND[g - 1] == "v":
                        dve.wait_ge(v_lo_ready, v_count(g))
                    else:
                        dve.wait_ge(qk_lo_ready, qk_count(g))
                    dve.tensor_tensor(pre[:, ::-1], bank[g % 3][:, :], r_all[:, :], ALU.mult).then_inc(acc_read, 1)

            def qkv_lo(g):
                t = QKV_TILE[g]
                if QKV_KIND[g] != "v":
                    dve.wait_ge(qk_hi_ready, qk_count(g) + 1)
                    dve.tensor_tensor(qk_lo[:, t, :], pre, qk_hi[:, t, :].bitcast(F32),
                                      ALU.subtract).then_inc(qk_lo_ready, 1)
                else:
                    dve.wait_ge(v_hi_ready, v_count(g) + 1)
                    dve.tensor_tensor(v_lo[:, t, :, 0::2, :],
                                      bank[5][:, :].rearrange("p (t e d) -> p t e d", t=QT, e=2),
                                      v_hi[:, t, :, 0::2, :].bitcast(F32),
                                      ALU.subtract).then_inc(v_lo_ready, 1)

            for g in range(N_QKV):
                if g:
                    qkv_lo(g - 1)
                qkv_main(g)
                if g == 2:
                    dve.wait_ge(tab_done, 1)
                    dve.tensor_copy(tab[:, 0:S], bank[7][0:NH, :]).then_inc(tab_copied, 1)
                    dve.tensor_copy(tab[:, S:N_TAB], bank[6][0:NH, :]).then_inc(tab_copied, 1)

            def scores_max(i, half):
                for qt in HALVES[half]:
                    n = order(i, qt)
                    k0, nk = key_tiles(i, qt)
                    dve.wait_ge(scores_done, n + 1)
                    if qt == 3:
                        dve.wait_ge(bias_arrived[i % 2], 16 * (i // 2 + 1))
                    dve.tensor_tensor_reduce(
                        out=probs[:, P_BASE[qt]:P_BASE[qt] + P * nk], in0=bank[2 + (n + 1) % 3][:, 0:P * nk],
                        in1=bias_m[:, i % 2, 0:P * nk], scale=1.0, scalar=-3e38,
                        op0=ALU.add, op1=ALU.max, accum_out=top[:, qt:qt + 1]).then_inc(max_ready, 1)
                a = HALVES[half][1]
                dve.wait_ge(max_ready, QT * i + 2 * half + 2)
                if i < 8:
                    dve.tensor_scalar(neg[:, a:a + 2], top[:, a:a + 2], par[:, C_SINK + i:C_SINK + i + 1],
                                      -1.0, ALU.max, ALU.mult).then_inc(neg_ready, 1)
                else:
                    dve.tensor_scalar(neg[:, a:a + 2], top[:, a:a + 2], -1.0, None,
                                      ALU.mult).then_inc(neg_ready, 1)

            def normalise(i, half):
                a = HALVES[half][1]
                dve.wait_ge(exp_ready, QT * i + 2 * half + 2)
                if i < 8:
                    dve.wait_ge(sink_ready, 2 * i + half + 1)
                    dve.tensor_tensor(den[:, a:a + 2], den[:, a:a + 2], sink_e[:, a:a + 2],
                                      ALU.add).then_inc(den_ready, 1)
                    dve.wait_ge(den_ready, 2 * i + half + 1)
                dve.reciprocal(rec[:, a:a + 2], den[:, a:a + 2]).then_inc(rec_ready, 1)
                dve.wait_ge(rec_ready, 2 * i + half + 1)
                for qt in HALVES[half]:
                    s = probs[:, P_BASE[qt]:P_BASE[qt] + P * key_tiles(i, qt)[1]]
                    dve.tensor_scalar(s, s, rec[:, qt:qt + 1], None, ALU.mult).then_inc(probs_ready, 1)

            def probs_t_lo(i, qt):
                n = order(i, qt)
                k0, nk = key_tiles(i, qt)
                dve.wait_ge(pt_hi_ready, n + 1)
                dve.tensor_tensor(pt_lo[:, k0:k0 + nk, P * qt:P * qt + P],
                                  bank[5 + n % 2][:, 0:P * nk].rearrange("p (k q) -> p k q", k=nk),
                                  pt_hi[:, k0:k0 + nk, P * qt:P * qt + P].bitcast(F32),
                                  ALU.subtract).then_inc(pt_lo_ready, 1)

            def gate_scale(j):
                dve.wait_ge(slab_done, G_GATE + j + 1)
                dve.tensor_tensor(store[:, j, :], bank[j % 2][:, :], r_all[:, :],
                                  ALU.mult).then_inc(acc_read, 1)

            scores_max(0, 0)
            scores_max(0, 1)
            normalise(0, 0)
            normalise(0, 1)
            qkv_lo(N_QKV - 1)
            gate_scale(0)
            for i in range(NH):
                probs_t_lo(i, 3)
                probs_t_lo(i, 2)
                if i + 1 < NH:
                    scores_max(i + 1, 0)
                probs_t_lo(i, 1)
                probs_t_lo(i, 0)
                if i + 1 < NH:
                    normalise(i + 1, 0)
                    scores_max(i + 1, 1)
                    normalise(i + 1, 1)
                    gate_scale(i + 1)
                if i % 2:
                    t = (Y_B + i // 2) if i < 8 else (Y_A + i // 2 - 4)
                    dve.wait_ge(y_hi_ready, i // 2 + 1)
                    dve.tensor_tensor(qk_lo[:, t, :], bank[7][:, :], qk_hi[:, t, :].bitcast(F32),
                                      ALU.subtract).then_inc(y_lo_ready, 1)

            for n in range(N_BRANCH):
                g = G_BRANCH + n
                dve.wait_ge(slab_done, g + 1)
                dve.wait_ge(gate_ready, 2 * n + 2)
                if n:
                    dve.wait_ge(m_lo_ready, n)
                dve.tensor_tensor(tmp_a, bank[2 * (n % 2) + 1][:, :], store[:, n, :],
                                  ALU.mult).then_inc(part_ready, 1)
                dve.tensor_tensor(tmp_b, bank[2 * (n % 2)][:, :], store[:, 8 + n, :],
                                  ALU.mult).then_inc(acc_read, 1)
                dve.wait_ge(part_ready, n + 1)
                dve.wait_ge(acc_read, g + 1)
                dve.tensor_tensor(tmp_a, tmp_a, tmp_b, ALU.add).then_inc(m_ready, 1)
                dve.wait_ge(m_hi_ready, n + 1)
                dve.tensor_tensor(x_lo[:, n, :], tmp_a, x_hi[:, n, :].bitcast(F32),
                                  ALU.subtract).then_inc(m_lo_ready, 1)

            for n in range(N_OUT):
                g = G_OUT + n
                dve.wait_ge(slab_done, g + 1)
                dve.wait_ge(x2_arrived[n], 16)
                dve.tensor_tensor(store[:, n, :], bank[4 + n % 2][:, :], store[:, n, :],
                                  ALU.add).then_inc(acc_read, 1)
                dve.memset(store[:, 8 + n, :], 0.0)
                dve.wait_ge(x1_hi_ready, n + 1)
                dve.scalar_tensor_tensor(out=qk_lo[:, n, :], in0=store[:, n, :],
                                         scalar=par[:, C_FFN + n:C_FFN + n + 1],
                                         in1=qk_hi[:, n, :].bitcast(F32), op0=ALU.mult,
                                         op1=ALU.subtract).then_inc(x1_lo_ready, 1)
                if n:
                    dve.wait_ge(x1sq_ready, n + 1)
                    if n > 1:
                        dve.wait_ge(x1sum_ready, n - 1)
                    dve.tensor_tensor(r_all[:, :], r_all[:, :], (tmp_a, tmp_b)[n % 2],
                                      ALU.add).then_inc(x1sum_ready, 1)

            def up(j, c):
                g = G_FF + j
                dve.wait_ge(relu_ready, c * 8 + (j + 1))
                if j:
                    dve.wait_ge(u_lo_ready, c * 8 + j)
                dve.tensor_tensor(tmp_b, tmp_a, tmp_a, ALU.mult).then_inc(acc_read, 1)
                dve.wait_ge(u_hi_ready, c * 8 + (j + 1))
                dve.tensor_tensor(x_lo[:, j, :], tmp_b, x_hi[:, j, :].bitcast(F32),
                                  ALU.subtract).then_inc(u_lo_ready, 1)

            with dve.Fori(0, CHUNKS - 1) as c:
                for j in range(8):
                    up(j, c)
                for n in range(8):
                    g = G_FF + 8 + n
                    dve.wait_ge(slab_done, c * PER_CHUNK + (g + 1))
                    dve.tensor_tensor(store[:, 8 + n, :], bank[g % 2][:, :], store[:, 8 + n, :],
                                      ALU.add).then_inc(acc_read, 1)
            dve.wait_ge(ms2_done, 1)
            dve.tensor_scalar(r_all[:, :], bank[6][:, :], EPS, None, ALU.add).then_inc(ms2_ready, 1)
            dve.wait_ge(ms2_ready, 1)
            dve.reciprocal(r_all[:, :], r_all[:, :]).then_inc(r2_ready, 1)
            for j in range(8):
                up(j, CHUNKS - 1)
            for n in range(8):
                g = N_SLABS - 8 + n
                o = store[:, 8 + n, :]
                dve.wait_ge(slab_done, g + 1)
                dve.tensor_tensor(o, bank[g % 2][:, :], o, ALU.add).then_inc(acc_read, 1)
                dve.wait_ge(acc_read, g + 1)
                dve.wait_ge(r2_ready, 1)
                dve.tensor_tensor(o, o, r_all[:, :], ALU.mult).then_inc(scaled_ready, 1)
                dve.wait_ge(scaled_ready, n + 1)
                dve.tensor_tensor(o, o, store[:, n, :], ALU.add).then_inc(out_ready, 1)

        @block.tensor
        def _(pe):
            def products(out_, pairs, start, stop):
                last = None
                for a, (wh, wl, xh, xl) in enumerate(pairs):
                    first, end = start and a == 0, stop and a == len(pairs) - 1
                    pe.matmul(out_, wh, xh, start=first, stop=False)
                    pe.matmul(out_, wh, xl, start=False, stop=False)
                    last = pe.matmul(out_, wl, xh, start=False, stop=end)
                return last

            def weight(g, kt):
                c = slice(P * kt, P * kt + P)
                return w_hi[:, g % WS, c], w_lo[:, g % WS, c]

            def slab_part(g, acc, moving, kts, start=True, stop=True):
                return products(acc[:, :], [weight(g, kt) + moving(kt) for kt in kts], start, stop)

            def from_x(kt):
                return x_hi[:, kt, :], x_lo[:, kt, :]

            def from_qk(kt):
                return qk_hi[:, kt, :], qk_lo[:, kt, :]

            def head_norm_sum(g):
                n = qk_count(g)
                pe.wait_ge(sq_ready, n + 1)
                if n >= 2:
                    pe.wait_ge(ss_read, n - 1)
                pe.matmul(bank[3 + n % 2][:, :], head_ones[:, :], sq, start=True, stop=True).then_inc(ss_done, 1)

            def v_transpose(g):
                pe.wait_ge(acc_read, g + 1)
                if v_count(g):
                    pe.wait_ge(v_lo_ready, v_count(g))
                for t in range(QT):
                    last = pe.transpose(bank[5][:, P * t:P * t + P], pre[:, P * t:P * t + P], ident[:, :])
                last.then_inc(vt_done, 1)

            def after(g):
                if QKV_KIND[g] == "v":
                    v_transpose(g)
                else:
                    head_norm_sum(g)

            pe.wait_ge(const_ready, 4)
            pe.wait_ge(ident_ready, 2)
            for g in range(N_QKV):
                pe.wait_ge(w_lo_ready, g + 1)
                if g >= 3:
                    pe.wait_ge(acc_read, g - 2)
                for kt in range(KT):
                    if g == 0:
                        pe.wait_ge(x_lo_ready, kt + 1)
                    last = slab_part(g, bank[g % 3], from_x, [kt], kt == 0, kt == KT - 1)
                    if g == 1 and kt == 1:
                        pe.wait_ge(xsum_ready, KT - 1)
                        pe.matmul(bank[6][:, :], ones[:, :], x_sum, start=True, stop=True).then_inc(ms_done, 1)
                    if g == 2 and kt == 1:
                        pe.wait_ge(tab_arrived, 32)
                        pe.wait_ge(ms_ready, 1)
                        pe.matmul(bank[7][0:NH, :], tabw, hot[:, 0:S], start=True, stop=True)
                        pe.matmul(bank[6][0:NH, :], tabw, hot[:, S:N_TAB], start=True,
                                  stop=True).then_inc(tab_done, 1)
                    if g and kt == 3:
                        after(g - 1)
                last.then_inc(slab_done, 1)

            def scores(i, qt):
                n = order(i, qt)
                rows = slice(HD * (i % 2), HD * (i % 2) + HD)
                q = (1 + i // 2) if i < 8 else (Y_A + i // 2 - 4)
                k = 0 if i < 8 else 5 + i // 2 - 4
                k0, nk = key_tiles(i, qt)
                qs, ks = slice(P * qt, P * qt + P), slice(P * k0, P * (k0 + nk))
                if n >= 3:
                    pe.wait_ge(max_ready, n - 2)
                last = products(bank[2 + (n + 1) % 3][:, 0:P * nk],
                                [(qk_hi[rows, q, qs], qk_lo[rows, q, qs], qk_hi[rows, k, ks], qk_lo[rows, k, ks])],
                                True, True)
                last.then_inc(scores_done, 1)

            def probs_transpose(i, qt):
                n = order(i, qt)
                pe.wait_ge(probs_ready, n + 1)
                if n >= 2:
                    pe.wait_ge(pt_lo_ready, n - 1)
                for j in range(key_tiles(i, qt)[1]):
                    at = P_BASE[qt] + P * j
                    last = pe.transpose(bank[5 + n % 2][:, P * j:P * j + P], probs[:, at:at + P], ident[:, :])
                last.then_inc(pt_done, 1)

            def values(i):
                pe.wait_ge(pt_lo_ready, QT * (i + 1))
                if i % 2 == 0 and i:
                    pe.wait_ge(y_lo_ready, i // 2)
                v = 0 if i < 8 else 1 + i // 2 - 4
                e = i % 2
                for kt in reversed(range(QT)):
                    q0 = P * (QT - 1 - kt)
                    q1 = min(S, q0 + 2 * P) if i < 8 else S
                    vh, vl = v_hi[:, v, kt, e:e + 2, :], v_lo[:, v, kt, e:e + 2, :]
                    vh, vl = vh.rearrange("p a d -> p (a d)"), vl.rearrange("p a d -> p (a d)")
                    ph, pl = pt_hi[:, kt, q0:q1], pt_lo[:, kt, q0:q1]
                    o = bank[7][:, q0:q1]
                    for w, m in ((vh, ph), (vh, pl), (vl, ph)):
                        last = pe.matmul(o, w, m, start=(e == 0 and kt == QT - 1 and w is vh and m is ph),
                                         stop=(e == 1 and kt == 0 and w is vl), skip_group_check=True)
                last.then_inc(pv_done, 1)

            def gate_part(j, kts, stop):
                g = G_GATE + j
                if kts[0] == 0:
                    pe.wait_ge(w_lo_ready, g + 1)
                    pe.wait_ge(acc_read, g - 2 if j < 2 else g - 1)
                last = slab_part(g, bank[j % 2], from_x, kts, kts[0] == 0, stop)
                if stop:
                    last.then_inc(slab_done, 1)

            pe.wait_ge(qk_lo_ready, N_QK)
            scores(0, 3)
            scores(0, 2)
            pe.wait_ge(acc_read, N_QKV)
            scores(0, 1)
            scores(0, 0)
            gate_part(0, [0, 1, 2], False)
            after(N_QKV - 1)
            gate_part(0, [3, 4, 5, 6, 7], True)
            pe.wait_ge(v_lo_ready, N_V)
            for i in range(NH):
                probs_transpose(i, 3)
                probs_transpose(i, 2)
                if i + 1 < NH:
                    scores(i + 1, 3)
                    scores(i + 1, 2)
                    gate_part(i + 1, [0, 1, 2], False)
                probs_transpose(i, 1)
                probs_transpose(i, 0)
                if i + 1 < NH:
                    scores(i + 1, 1)
                    scores(i + 1, 0)
                    gate_part(i + 1, [3, 4, 5, 6, 7], True)
                    values(i)

            def from_y(kt):
                return from_qk(Y_B + kt if kt < 4 else Y_A + kt - 4)

            for n in range(N_BRANCH):
                g = G_BRANCH + n
                pe.wait_ge(w_lo_ready, g + 1)
                pe.wait_ge(acc_read, g if n < 2 else g - 1)
                slab_part(g, bank[2 * (n % 2)], from_y, [0, 1, 2, 3])
                if n == 0:
                    values(NH - 1)
                    pe.wait_ge(y_lo_ready, 7)
                    slab_part(g, bank[1], from_y, [4, 5, 6], True, False)
                    pe.wait_ge(y_lo_ready, 8)
                    last = slab_part(g, bank[1], from_y, [7], False, True)
                else:
                    last = slab_part(g, bank[2 * (n % 2) + 1], from_y, [4, 5, 6, 7])
                last.then_inc(slab_done, 1)

            for n in range(N_OUT):
                g = G_OUT + n
                pe.wait_ge(w_lo_ready, g + 1)
                if n >= 2:
                    pe.wait_ge(acc_read, g - 1)
                for kt in range(KT):
                    if n == 0:
                        pe.wait_ge(m_lo_ready, kt + 1)
                    last = slab_part(g, bank[4 + n % 2], from_x, [kt], kt == 0, kt == KT - 1)
                last.then_inc(slab_done, 1)

            def feed_forward(c, first=False):
                at = c * PER_CHUNK
                for j in range(8):
                    g = G_FF + j
                    pe.wait_ge(w_lo_ready, at + (g + 1))
                    pe.wait_ge(acc_read, at + (g - 1))
                    for kt in range(KT):
                        if j == 0:
                            pe.wait_ge(x1_lo_ready, kt + 1)
                        last = slab_part(g, bank[g % 2], from_qk, [kt], kt == 0, kt == KT - 1)
                    last.then_inc(slab_done, 1)
                for n in range(8):
                    g = G_FF + 8 + n
                    pe.wait_ge(w_lo_ready, at + (g + 1))
                    pe.wait_ge(acc_read, at + (g - 1))
                    for kt in range(KT):
                        if n == 0:
                            pe.wait_ge(u_lo_ready, c * 8 + (kt + 1))
                        last = slab_part(g, bank[g % 2], from_x, [kt], kt == 0, kt == KT - 1)
                    last.then_inc(slab_done, 1)

            with pe.Fori(0, CHUNKS - 1) as c:
                feed_forward(c)
            pe.wait_ge(x1sum_ready, N_OUT - 1)
            pe.matmul(bank[6][:, :], ones[:, :], r_all[:, :], start=True, stop=True).then_inc(ms2_done, 1)
            feed_forward(CHUNKS - 1)


def rel_bucket(n):
    n = np.maximum(n, 0)
    exact = NBUCKET // 2
    nf = np.maximum(n, 1).astype(np.float32)
    large = exact + (np.log(nf / np.float32(exact)) / np.float32(np.log(MAXDIST / exact))
                     * np.float32(NBUCKET - exact)).astype(np.int32)
    return np.where(n < exact, n, np.minimum(large, NBUCKET - 1))


def distance_onehot():
    hot = np.zeros((NBUCKET + 1, N_TAB), np.float32)
    for at, n, limit in ((T_A, T_B, S), (T_B, N_TAB - T_B, WINDOW)):
        d = np.arange(n) - (P - 1)
        row = np.where((d >= 0) & (d < limit), rel_bucket(d), NBUCKET)
        hot[row, at + np.arange(n)] = 1.0
    return hot


def as_slabs(w):
    n = w.shape[1] // P
    return w.reshape(KT, P, n, P).transpose(2, 1, 0, 3).reshape(n, P, D)


def kernel(**inputs):
    import concourse.bacc as bacc
    from concourse.bass_utils import run_bass_kernel_spmd

    a = {k: np.asarray(v) for k, v in inputs.items()}
    order_b = [t + 4 * e for t in range(4) for e in range(2)]
    w_in = a["w_in"][0]
    wa = 8 * HD
    at = np.cumsum([0, wa, wa, wa, wa, 2 * HD, 2 * HD, D])
    qa, ka, va, qb, kb, vb, ga, gb = (w_in[:, i:j] for i, j in zip(at, [*at[1:], w_in.shape[1]]))
    qb = qb.reshape(D, 8, HD)[:, order_b].reshape(D, wa)
    ka, qa = ka.reshape(D, 4, P), qa.reshape(D, 4, P)
    kq = [t[:, p] for p in range(4) for t in (ka, qa)]
    w_qkv = np.concatenate([kb, qb, vb, *kq, va, ga, gb], axis=1)
    branch_b = a["w_branch_b"][0].reshape(8, HD, D)[order_b].reshape(wa, D)
    w_branch = np.concatenate([branch_b, a["w_branch_a"][0]], axis=0)
    ff1 = as_slabs(a["w_ff1"][0]).reshape(CHUNKS, 8, P, D)
    ff2 = np.stack([as_slabs(w) for w in a["w_ff2"][0].reshape(CHUNKS, D, D)])
    slabs = np.concatenate([as_slabs(w_qkv), as_slabs(w_branch), as_slabs(a["w_out"][0]),
                            np.concatenate([ff1, ff2], axis=1).reshape(CHUNKS * PER_CHUNK, P, D)])

    def columns(v):
        return v.reshape(-1, P).T

    def twice(v):
        return np.tile(v.reshape(-1, 1), (2, 1))

    params = np.concatenate(
        [columns(a["g_mix"]), columns(a["g_ffn"]), columns(a["b_gate"]), twice(a["k_norm_b"]),
         twice(a["q_norm_b"]), twice(a["k_norm_a"]), twice(a["q_norm_a"]),
         np.tile(a["sinks"].reshape(1, 8)[:, order_b], (P, 1))], axis=1)
    table = np.concatenate([a["rel_bias"][:, 8:][:, order_b], a["rel_bias"][:, :8]], axis=1)
    arrays = {
        "x_t": a["x"].reshape(S, D).T.reshape(KT, P, S),
        "slabs": slabs, "params": params, "table": table, "onehot": distance_onehot(),
    }
    arrays = {k: np.ascontiguousarray(v) for k, v in arrays.items()}
    nc = bacc.Bacc("TRN2", target_bir_lowering=False, num_devices=1)
    F32 = mybir.dt.float32
    aps = [nc.dram_tensor(k, v.shape, F32, kind="ExternalInput").ap() for k, v in arrays.items()]
    tab_dram = nc.dram_tensor("tab_dram", (NH, N_TAB), F32, kind="Internal").ap()
    out = nc.dram_tensor("out", (KT, P, S), F32, kind="ExternalOutput").ap()
    build(nc, *aps, tab_dram, out)
    r = run_bass_kernel_spmd(nc, [arrays], core_ids=[0])
    return r.results[0]["out"].reshape(D, S).T.reshape(1, S, D)
```

```python
import numpy as np
import concourse.bass as bass
from concourse import mybir
from contextlib import ExitStack

D, S, HD, DFF = 1024, 512, 64, 4096
P = 128
KT = D // P
QT = S // P
NBUCKET, MAXDIST, WINDOW = 32, 2048, 128
EPS = 1e-6
MASK = -1e30
NH = 16

KV_B, V_B = 0, 5
N_QKV, N_GATE, N_BRANCH, N_OUT = 18, 16, 8, 8
G_GATE = N_QKV
G_BRANCH = G_GATE + N_GATE
G_OUT = G_BRANCH + N_BRANCH
G_FF = G_OUT + N_OUT
CHUNKS = 4
PER_CHUNK = 16
N_SLABS = G_FF + CHUNKS * PER_CHUNK
RAW, WS = 4, 2

QKV_KIND = ["k", "q", "q", "q", "q", "v"] + ["k", "q"] * 4 + ["v"] * 4
QKV_TILE = [0, 1, 2, 3, 4, 0] + [5, 9, 6, 10, 7, 11, 8, 12] + [1, 2, 3, 4]
Y_B, Y_A = 1, 9
C_MIX, C_FFN, C_BGATE, C_NORM, C_SINK, N_PAR = 0, 8, 16, 32, 36, 44
T_A, T_B, N_TAB = 0, 640, 1024
P_BASE = [0, 128, 384, 768]


def norm_column(slab):
    return C_NORM + (0 if slab < V_B else 2) + (QKV_KIND[slab] == "q")


def build(nc, x_t, slabs, params, table, onehot, tab_dram, out):
    F32, R = mybir.dt.float32, mybir.dt.float32r
    ALU, ACT = mybir.AluOpType, mybir.ActivationFunctionType
    ctx = ExitStack()
    with ctx:
        def sb(name, shape, dt):
            return ctx.enter_context(nc.sbuf_tensor(name, shape, dt))

        def sem(name):
            return ctx.enter_context(nc.semaphore(name))

        w_raw = sb("w_raw", [P, RAW, D], F32)
        w_hi, w_lo = sb("w_hi", [P, WS, D], R), sb("w_lo", [P, WS, D], R)
        x_hi, x_lo = sb("x_hi", [P, KT, S], R), sb("x_lo", [P, KT, S], R)
        qk_hi, qk_lo = sb("qk_hi", [P, 13, S], R), sb("qk_lo", [P, 13, S], R)
        v_hi, v_lo = sb("v_hi", [P, 5, QT, 3, HD], R), sb("v_lo", [P, 5, QT, 3, HD], R)
        store = sb("store", [P, 16, S], F32)
        pt_hi, pt_lo = sb("pt_hi", [P, QT, S], R), sb("pt_lo", [P, QT, S], R)
        probs = sb("probs", [P, 1280], F32)
        bias_m = sb("bias_m", [P, 2, S], F32)
        r_all = sb("r_all", [P, S], F32)
        ident = sb("ident", [P, P], F32)
        ones = sb("ones", [P, 1], F32)
        head_cols = sb("head_cols", [P, 2], F32)
        ms_tok, eps_tok, r_tok = sb("ms_tok", [P, QT], F32), sb("eps_tok", [P, QT], F32), sb("r_tok", [P, QT], F32)
        ss_tok, ssi_tok, root_tok, fix_tok = (sb(n, [P, 2 * QT], F32) for n in
                                              ("ss_tok", "ssi_tok", "root_tok", "fix_tok"))
        par = sb("par", [P, N_PAR], F32)
        top = sb("top", [P, QT], F32)
        neg = sb("neg", [P, QT], F32)
        den = sb("den", [P, QT], F32)
        sink_e = sb("sink_e", [P, QT], F32)
        rec = sb("rec", [P, QT], F32)
        bank = [ctx.enter_context(nc.psum_tensor(f"bank{i}", [P, 512], F32)) for i in range(8)]

        xsq = [store[:, 8, :], store[:, 9, :]]
        tab = store[0:NH, 10:12, :].rearrange("p a n -> p (a n)")
        x_sum = store[:, 12, :]
        pre_v = store[:, 12, :]
        pre = store[:, 13, :]
        sq = store[:, 14, :]
        inv = store[:, 15, :]
        inv_tok = store[:, 8, :]
        hot = probs[0:NBUCKET + 1, 0:N_TAB]
        tabw = probs[0:NBUCKET + 1, N_TAB:N_TAB + NH]
        tmp_a, tmp_b = probs[:, 0:S], probs[:, S:2 * S]

        arrived = [sem(f"slab_arrived{i}") for i in range(RAW)]
        x_arrived = [sem(f"x_arrived{i}") for i in range(KT)]
        par_arrived = sem("par_arrived")
        tab_arrived = sem("tab_arrived")
        tab_stored = sem("tab_stored")
        bias_arrived = [sem("bias_arrived0"), sem("bias_arrived1")]
        out_stored = sem("out_stored")
        const_ready, ident_ready = sem("const_ready"), sem("ident_ready")
        par_ready = sem("par_ready")
        w_hi_ready, w_lo_ready = sem("w_hi_ready"), sem("w_lo_ready")
        slab_done = sem("slab_done")
        acc_read = sem("acc_read")
        x_hi_ready, x_lo_ready = sem("x_hi_ready"), sem("x_lo_ready")
        xsq_ready, xsum_ready = sem("xsq_ready"), sem("xsum_ready")
        w0_lo_ready = sem("w0_lo_ready")
        ms_done, ms_ready, r_sqrt, r_ready = sem("ms_done"), sem("ms_ready"), sem("r_sqrt"), sem("r_ready")
        r_spread = sem("r_spread")
        tab_done, tab_copied = sem("tab_done"), sem("tab_copied")
        pre_ready, pre_v_ready = sem("pre_ready"), sem("pre_v_ready")
        sq_ready, ss_done, ss_read = sem("sq_ready"), sem("ss_done"), sem("ss_read")
        ss_inv, root_ready = sem("ss_inv"), sem("root_ready")
        fix_ready, inv_ready = sem("fix_ready"), sem("inv_ready")
        spread_done, spread_ready = sem("spread_done"), sem("spread_ready")
        qk_hi_ready, qk_lo_ready = sem("qk_hi_ready"), sem("qk_lo_ready")
        vt_done, v_hi_ready, v_lo_ready = sem("vt_done"), sem("v_hi_ready"), sem("v_lo_ready")
        scores_done, max_ready, neg_ready = sem("scores_done"), sem("max_ready"), sem("neg_ready")
        exp_ready, sink_ready = sem("exp_ready"), sem("sink_ready")
        den_ready, rec_ready, probs_ready = sem("den_ready"), sem("rec_ready"), sem("probs_ready")
        pt_done, pt_hi_ready, pt_lo_ready = sem("pt_done"), sem("pt_hi_ready"), sem("pt_lo_ready")
        pv_done, y_hi_ready, y_lo_ready = sem("pv_done"), sem("y_hi_ready"), sem("y_lo_ready")
        gate_ready = sem("gate_ready")
        part_ready, m_ready = sem("part_ready"), sem("m_ready")
        m_hi_ready, m_lo_ready = sem("m_hi_ready"), sem("m_lo_ready")
        x2_arrived = [sem(f"x2_arrived{i}") for i in range(KT)]
        x1_hi_ready, x1_lo_ready = sem("x1_hi_ready"), sem("x1_lo_ready")
        x1sq_ready, x1sum_ready = sem("x1sq_ready"), sem("x1sum_ready")
        ms2_done, ms2_ready, r2_ready = sem("ms2_done"), sem("ms2_ready"), sem("r2_ready")
        r2_spread, r2_all_ready = sem("r2_spread"), sem("r2_all_ready")
        relu_ready, u_hi_ready, u_lo_ready = sem("relu_ready"), sem("u_hi_ready"), sem("u_lo_ready")
        sum_ready, scaled_ready, out_ready = sem("sum_ready"), sem("scaled_ready"), sem("out_ready")

        def qk_count(slab):
            return sum(kind != "v" for kind in QKV_KIND[:slab])

        def v_count(slab):
            return sum(kind == "v" for kind in QKV_KIND[:slab])

        def read(g):
            return g - N_QKV + 1

        N_QK, N_V = qk_count(N_QKV), v_count(N_QKV)

        def key_tiles(i, qt):
            return QT - 1 - qt, min(2, qt + 1) if i < 8 else qt + 1

        def order(i, qt):
            return QT * i + (QT - 1 - qt)

        HALVES = [(3, 2), (1, 0)]

        block = ctx.enter_context(nc.Block())

        @block.sync
        def _(sp):
            def load_slab(g):
                if g >= RAW:
                    if g > RAW:
                        sp.wait_ge(w_lo_ready, g - RAW)
                    else:
                        sp.wait_ge(w0_lo_ready, 2)
                sp.dma_start(w_raw[:, g % RAW, :], slabs[g]).then_inc(arrived[g % RAW], 16)

            def load_bias(i):
                if i >= 2:
                    sp.wait_ge(max_ready, QT * (i - 1))
                else:
                    sp.wait_ge(tab_stored, 16)
                at, n = (T_B, 2 * P) if i < 8 else (T_A, S)
                src = bass.AP(tensor=tab_dram.tensor, offset=i * N_TAB + at, ap=[[1, P], [1, n]])
                sp.dma_start(bias_m[:, i % 2, 0:n], src).then_inc(bias_arrived[i % 2], 16)

            sp.dma_start(par[:, :], params).then_inc(par_arrived, 16)
            for k in range(KT):
                sp.dma_start(store[:, k, :], x_t[k]).then_inc(x_arrived[k], 16)
                if k == 0:
                    load_slab(0)
                if k == 3:
                    load_slab(1)
            sp.dma_start(hot, onehot).then_inc(tab_arrived, 16)
            sp.dma_start(tabw[0:NBUCKET, :], table).then_inc(tab_arrived, 16)
            for g in range(2, G_FF):
                if g == 14:
                    sp.wait_ge(tab_copied, 2)
                    sp.dma_start(tab_dram, tab).then_inc(tab_stored, 16)
                if g == 16:
                    load_bias(0)
                    load_bias(1)
                if 2 <= g - 22 < NH:
                    load_bias(g - 22)
                if G_BRANCH + 6 <= g < G_OUT + 6:
                    n = g - G_BRANCH - 6
                    sp.wait_ge(acc_read, read(G_BRANCH + n))
                    sp.dma_start(store[:, n, :], x_t[n]).then_inc(x2_arrived[n], 16)
                load_slab(g)
            with sp.Fori(0, CHUNKS) as c:
                for k in range(PER_CHUNK):
                    g = sp.snap(c * PER_CHUNK + (G_FF + k))
                    sp.wait_ge(w_lo_ready, c * PER_CHUNK + (G_FF + k - RAW))
                    sp.dma_start(w_raw[:, (G_FF + k) % RAW, :],
                                 slabs[bass.ds(g, 1)].rearrange("a p n -> (a p) n")
                                 ).then_inc(arrived[(G_FF + k) % RAW], 16)
            for n in range(KT):
                sp.wait_ge(out_ready, n + 1)
                sp.dma_start(out[n], store[:, 8 + n, :]).then_inc(out_stored, 16)
            sp.wait_ge(out_stored, 16 * KT)

        @block.gpsimd
        def _(pool):
            pool.memset(ident[:, :], 0.0).then_inc(ident_ready, 1)
            pool.wait_ge(ident_ready, 1)
            pool.affine_select(out=ident[:, :], in_=ident[:, :], compare_op=ALU.not_equal, fill=1.0,
                               base=0, pattern=[[-1, P]], channel_multiplier=1).then_inc(ident_ready, 1)

            def split_lo(g, count):
                pool.wait_ge(w_hi_ready, count)
                pool.tensor_tensor(w_lo[:, g % WS, :], w_raw[:, g % RAW, :],
                                   w_hi[:, g % WS, :].bitcast(F32), ALU.subtract).then_inc(w_lo_ready, 1)

            split_lo(1, 3)
            with pool.Fori(0, (N_SLABS - 2) // RAW) as c:
                for k in range(RAW):
                    split_lo(2 + k, c * RAW + (2 + k + 2))

        @block.scalar
        def _(act):
            def split_hi(g, c=None):
                at = 0 if c is None else c * PER_CHUNK
                act.wait_ge(arrived[g % RAW], 16 * (g // RAW + 1) + (0 if c is None else c * (16 * PER_CHUNK // RAW)))
                if g >= WS:
                    act.wait_ge(slab_done, at + (g - WS + 1))
                act.activation(w_hi[:, g % WS, :], w_raw[:, g % RAW, :], ACT.Copy).then_inc(w_hi_ready, 1)

            act.wait_ge(const_ready, 1)
            act.activation(sink_e[:, 0:1], ones[:, :], ACT.Sqrt)
            act.wait_ge(par_arrived, 16)
            for k in range(KT):
                if k == 1 or k == 2:
                    half = slice((k - 1) * D // 2, k * D // 2)
                    act.wait_ge(arrived[0], 16)
                    act.activation(w_hi[:, 0, half], w_raw[:, 0, half], ACT.Copy).then_inc(w_hi_ready, 1)
                if k == 5:
                    split_hi(1)
                act.wait_ge(x_arrived[k], 16)
                act.activation(x_hi[:, k, :], store[:, k, :], ACT.Copy,
                               scale=par[:, C_MIX + k:C_MIX + k + 1]).then_inc(x_hi_ready, 1)
            for k in range(KT):
                if k >= 3:
                    act.wait_ge(xsum_ready, k - 2)
                act.activation(xsq[k % 2] if k else x_sum, store[:, k, :], ACT.Square).then_inc(xsq_ready, 1)

            def qkv_square(g):
                if QKV_KIND[g] != "v":
                    n = qk_count(g)
                    act.wait_ge(slab_done, g + 1)
                    if n:
                        act.wait_ge(ss_done, n)
                    act.activation(sq, bank[g % 3][:, :], ACT.Square).then_inc(sq_ready, 1)

            def qkv_spread(g):
                if QKV_KIND[g] != "v":
                    n = qk_count(g)
                    act.wait_ge(spread_done, n + 1)
                    if n:
                        act.wait_ge(pre_ready, n)
                    act.activation(inv, bank[3 + n % 2][:, :], ACT.Copy).then_inc(spread_ready, 1)

            def qkv_hi(g):
                t = QKV_TILE[g]
                if QKV_KIND[g] != "v":
                    act.wait_ge(pre_ready, qk_count(g) + 1)
                    act.activation(qk_hi[:, t, :], pre, ACT.Copy).then_inc(qk_hi_ready, 1)
                else:
                    act.wait_ge(vt_done, v_count(g) + 1)
                    if v_count(g) == 0:
                        act.wait_ge(const_ready, 4)
                    act.activation(v_hi[:, t, :, 0::2, :],
                                   bank[5][:, :].rearrange("p (t e d) -> p t e d", t=QT, e=2),
                                   ACT.Copy).then_inc(v_hi_ready, 1)

            def qkv_sqrt(g):
                if QKV_KIND[g] != "v":
                    n = qk_count(g)
                    act.wait_ge(ss_inv, n + 1)
                    act.activation(root_tok[:, :], ssi_tok[:, :], ACT.Sqrt).then_inc(root_ready, 1)

            for g in range(N_QKV):
                if g and QKV_KIND[g - 1] == "v":
                    qkv_hi(g - 1)
                split_hi(g + 2)
                qkv_square(g)
                if g and QKV_KIND[g - 1] != "v":
                    qkv_spread(g - 1)
                    qkv_hi(g - 1)
                if g == 0:
                    act.wait_ge(ms_ready, 3)
                    act.activation(r_tok[:, :], ms_tok[:, :], ACT.Sqrt).then_inc(r_sqrt, 1)
                if g == 2:
                    act.wait_ge(r_spread, 1)
                    act.activation(r_all[:, :], bank[6][:, :], ACT.Copy).then_inc(r_ready, 1)
                qkv_sqrt(g)

            def exps(i, half):
                act.wait_ge(neg_ready, 2 * i + half + 1)
                for qt in HALVES[half]:
                    n = P * key_tiles(i, qt)[1]
                    s = probs[:, P_BASE[qt]:P_BASE[qt] + n]
                    act.activation(s, s, ACT.Exp, bias=neg[:, qt:qt + 1],
                                   accum_out=den[:, qt:qt + 1]).then_inc(exp_ready, 1)
                if i < 8:
                    a = HALVES[half][1]
                    act.activation(sink_e[:, a:a + 2], neg[:, a:a + 2], ACT.Exp,
                                   bias=par[:, C_SINK + i:C_SINK + i + 1]).then_inc(sink_ready, 1)

            def probs_t_hi(i, qt):
                n = order(i, qt)
                k0, nk = key_tiles(i, qt)
                act.wait_ge(pt_done, n + 1)
                act.activation(pt_hi[:, k0:k0 + nk, P * qt:P * qt + P],
                               bank[6 - n % 2][:, 0:P * nk].rearrange("p (k q) -> p k q", k=nk),
                               ACT.Copy).then_inc(pt_hi_ready, 1)

            exps(0, 0)
            qkv_hi(N_QKV - 1)
            exps(0, 1)
            for i in range(NH):
                probs_t_hi(i, 3)
                probs_t_hi(i, 2)
                split_hi(G_GATE + 2 + i)
                if i + 1 < NH:
                    exps(i + 1, 0)
                probs_t_hi(i, 1)
                probs_t_hi(i, 0)
                if i + 1 < NH:
                    exps(i + 1, 1)
                if i % 2:
                    act.wait_ge(pv_done, i + 1)
                    act.activation(qk_hi[:, (Y_B + i // 2) if i < 8 else (Y_A + i // 2 - 4), :],
                                   bank[7][:, :], ACT.Copy).then_inc(y_hi_ready, 1)

            def gate(n):
                for j in (n, 8 + n):
                    act.wait_ge(acc_read, read(G_GATE + j))
                    act.activation(store[:, j, :], store[:, j, :], ACT.Sigmoid,
                                   bias=par[:, C_BGATE + j:C_BGATE + j + 1]).then_inc(gate_ready, 1)

            gate(0)
            for n in range(N_BRANCH):
                split_hi(G_BRANCH + n + 2)
                if n + 1 < N_BRANCH:
                    gate(n + 1)
                act.wait_ge(m_ready, n + 1)
                act.activation(x_hi[:, n, :], tmp_a, ACT.Copy).then_inc(m_hi_ready, 1)

            for n in range(N_OUT):
                act.wait_ge(acc_read, read(G_OUT + n))
                act.activation(qk_hi[:, n, :], store[:, n, :], ACT.Copy,
                               scale=par[:, C_FFN + n:C_FFN + n + 1]).then_inc(x1_hi_ready, 1)
                split_hi(G_OUT + n + 2)
                if n >= 3:
                    act.wait_ge(x1sum_ready, n - 2)
                act.activation((tmp_a, tmp_b)[n % 2] if n else r_all[:, :], store[:, n, :],
                               ACT.Square).then_inc(x1sq_ready, 1)

            def up(j, c, last=False):
                g = G_FF + j
                at = c * PER_CHUNK
                act.wait_ge(slab_done, at + (g + 1))
                act.activation(tmp_a, bank[g % 2][:, :], ACT.Relu).then_inc(relu_ready, 1)
                if isinstance(c, int):
                    split_hi(g + 2 + c * PER_CHUNK)
                else:
                    split_hi(g + 2, c)
                act.wait_ge(acc_read, at + read(g))
                act.activation(x_hi[:, j, :], tmp_b, ACT.Copy).then_inc(u_hi_ready, 1)

            act.wait_ge(x1sum_ready, N_OUT - 1)
            with act.Fori(0, CHUNKS - 1) as c:
                for j in range(8):
                    up(j, c)
                for n in range(8):
                    split_hi(G_FF + 8 + n + 2, c)
            for j in range(8):
                up(j, CHUNKS - 1)
                if j == 3:
                    act.wait_ge(r2_spread, 1)
                    act.activation(r_all[:, :], bank[7][:, :], ACT.Copy).then_inc(r2_all_ready, 1)
            for n in range(6):
                split_hi(N_SLABS - 8 + n + 2)

        @block.vector
        def _(dve):
            dve.memset(ones[:, :], 1.0 / D).then_inc(const_ready, 1)
            dve.memset(v_hi[:, :, :, 1, :].bitcast(F32), 0.0)
            dve.memset(v_lo[:, :, :, 1, :].bitcast(F32), 0.0).then_inc(const_ready, 1)
            for a in range(2):
                for b in range(2):
                    last = dve.memset(head_cols[HD * a:HD * (a + 1), b:b + 1], 1.0 / HD if a == b else 0.0)
            last.then_inc(const_ready, 1)
            dve.memset(tabw[NBUCKET:NBUCKET + 1, :], MASK).then_inc(const_ready, 1)
            dve.wait_ge(par_arrived, 16)
            for a in (1, 3):
                col = par[:, C_NORM + a:C_NORM + a + 1]
                dve.tensor_scalar(col, col, HD ** -0.5, None, ALU.mult).then_inc(par_ready, 1)
            for k in range(KT):
                if k == 1 or k == 2:
                    half = slice((k - 1) * D // 2, k * D // 2)
                    dve.wait_ge(w_hi_ready, k)
                    dve.tensor_tensor(w_lo[:, 0, half], w_raw[:, 0, half], w_hi[:, 0, half].bitcast(F32),
                                      ALU.subtract).then_inc(w0_lo_ready, 1)
                dve.wait_ge(x_hi_ready, k + 1)
                dve.scalar_tensor_tensor(out=x_lo[:, k, :], in0=store[:, k, :],
                                         scalar=par[:, C_MIX + k:C_MIX + k + 1],
                                         in1=x_hi[:, k, :].bitcast(F32), op0=ALU.mult,
                                         op1=ALU.subtract).then_inc(x_lo_ready, 1)
            for k in range(1, KT):
                dve.wait_ge(xsq_ready, k + 1)
                if k > 1:
                    dve.wait_ge(xsum_ready, k - 1)
                dve.tensor_tensor(x_sum, x_sum, xsq[k % 2], ALU.add).then_inc(xsum_ready, 1)
            dve.wait_ge(ms_done, 1)
            dve.tensor_scalar(ms_tok[:, :], bank[6][:, 0:QT], EPS, None, ALU.add).then_inc(ms_ready, 1)
            dve.wait_ge(ms_ready, 1)
            dve.tensor_scalar(eps_tok[:, :], ms_tok[:, :], EPS, None, ALU.mult).then_inc(ms_ready, 1)
            dve.wait_ge(ms_ready, 2)
            dve.reciprocal(ms_tok[:, :], ms_tok[:, :]).then_inc(ms_ready, 1)

            def qk_factor(g):
                if QKV_KIND[g] != "v":
                    n = qk_count(g)
                    dve.wait_ge(ss_done, n + 1)
                    if n:
                        dve.wait_ge(inv_ready, n)
                    dve.tensor_tensor(ss_tok[:, :].rearrange("p (t e) -> p t e", e=2), bank[3 + n % 2][:, 0:2 * QT].rearrange("p (t e) -> p t e", e=2),
                                      eps_tok[:, :].unsqueeze(2).to_broadcast([P, QT, 2]),
                                      ALU.add).then_inc(ss_read, 1)
                    dve.wait_ge(ss_read, n + 1)
                    dve.reciprocal(ssi_tok[:, :], ss_tok[:, :]).then_inc(ss_inv, 1)

            def qk_refine(g):
                if QKV_KIND[g] != "v":
                    n = qk_count(g)
                    dve.wait_ge(root_ready, n + 1)
                    dve.tensor_tensor(fix_tok[:, :], root_tok[:, :], root_tok[:, :], ALU.mult).then_inc(fix_ready, 1)
                    dve.wait_ge(fix_ready, 3 * n + 1)
                    dve.tensor_tensor(fix_tok[:, :], fix_tok[:, :], ss_tok[:, :], ALU.mult).then_inc(fix_ready, 1)
                    dve.wait_ge(fix_ready, 3 * n + 2)
                    dve.tensor_scalar(fix_tok[:, :], fix_tok[:, :], -0.5, 1.5, ALU.mult, ALU.add).then_inc(fix_ready, 1)
                    dve.wait_ge(fix_ready, 3 * n + 3)
                    if n:
                        dve.wait_ge(spread_done, n)
                    dve.tensor_tensor(inv_tok.rearrange("p (h d) -> p h d", d=HD),
                                      fix_tok[:, :].unsqueeze(2).to_broadcast([P, 2 * QT, HD]),
                                      root_tok[:, :].unsqueeze(2).to_broadcast([P, 2 * QT, HD]),
                                      ALU.mult).then_inc(inv_ready, 1)

            def qk_norm(g):
                if QKV_KIND[g] != "v":
                    n = qk_count(g)
                    dve.wait_ge(spread_ready, n + 1)
                    if n:
                        dve.wait_ge(qk_lo_ready, n)
                    dve.wait_ge(par_ready, 2)
                    c = norm_column(g)
                    to = pre[:, ::-1] if QKV_KIND[g] == "k" else pre
                    dve.scalar_tensor_tensor(out=to, in0=bank[g % 3][:, :], scalar=par[:, c:c + 1],
                                             in1=inv, op0=ALU.mult, op1=ALU.mult).then_inc(pre_ready, 1)

            def v_scale(g):
                if QKV_KIND[g] == "v":
                    n = v_count(g)
                    dve.wait_ge(slab_done, g + 1)
                    dve.wait_ge(r_ready, 1)
                    if n:
                        dve.wait_ge(v_lo_ready, n)
                    dve.tensor_tensor(pre_v[:, ::-1], bank[g % 3][:, :], r_all[:, :], ALU.mult).then_inc(pre_v_ready, 1)

            def qkv_lo(g):
                t = QKV_TILE[g]
                if QKV_KIND[g] != "v":
                    dve.wait_ge(qk_hi_ready, qk_count(g) + 1)
                    dve.tensor_tensor(qk_lo[:, t, :], pre, qk_hi[:, t, :].bitcast(F32),
                                      ALU.subtract).then_inc(qk_lo_ready, 1)
                else:
                    dve.wait_ge(v_hi_ready, v_count(g) + 1)
                    dve.tensor_tensor(v_lo[:, t, :, 0::2, :],
                                      bank[5][:, :].rearrange("p (t e d) -> p t e d", t=QT, e=2),
                                      v_hi[:, t, :, 0::2, :].bitcast(F32),
                                      ALU.subtract).then_inc(v_lo_ready, 1)

            for g in range(N_QKV):
                if g:
                    qk_norm(g - 1)
                    if QKV_KIND[g - 1] == "v":
                        qkv_lo(g - 1)
                v_scale(g)
                qk_factor(g)
                if g and QKV_KIND[g - 1] != "v":
                    qkv_lo(g - 1)
                qk_refine(g)
                if g == 5:
                    dve.wait_ge(tab_done, 1)
                    dve.tensor_copy(tab[:, 0:S], bank[7][0:NH, :]).then_inc(tab_copied, 1)
                    dve.tensor_copy(tab[:, S:N_TAB], bank[6][0:NH, :]).then_inc(tab_copied, 1)

            def scores_max(i, half):
                for qt in HALVES[half]:
                    n = order(i, qt)
                    k0, nk = key_tiles(i, qt)
                    dve.wait_ge(scores_done, n + 1)
                    if qt == 3:
                        dve.wait_ge(bias_arrived[i % 2], 16 * (i // 2 + 1))
                    dve.tensor_tensor_reduce(
                        out=probs[:, P_BASE[qt]:P_BASE[qt] + P * nk], in0=bank[2 + (n + 1) % 3][:, 0:P * nk],
                        in1=bias_m[:, i % 2, 0:P * nk], scale=1.0, scalar=-3e38,
                        op0=ALU.add, op1=ALU.max, accum_out=top[:, qt:qt + 1]).then_inc(max_ready, 1)
                a = HALVES[half][1]
                dve.wait_ge(max_ready, QT * i + 2 * half + 2)
                if i < 8:
                    dve.tensor_scalar(neg[:, a:a + 2], top[:, a:a + 2], par[:, C_SINK + i:C_SINK + i + 1],
                                      -1.0, ALU.max, ALU.mult).then_inc(neg_ready, 1)
                else:
                    dve.tensor_scalar(neg[:, a:a + 2], top[:, a:a + 2], -1.0, None,
                                      ALU.mult).then_inc(neg_ready, 1)

            def normalise(i, half):
                a = HALVES[half][1]
                dve.wait_ge(exp_ready, QT * i + 2 * half + 2)
                if i < 8:
                    dve.wait_ge(sink_ready, 2 * i + half + 1)
                    dve.tensor_tensor(den[:, a:a + 2], den[:, a:a + 2], sink_e[:, a:a + 2],
                                      ALU.add).then_inc(den_ready, 1)
                    dve.wait_ge(den_ready, 2 * i + half + 1)
                dve.reciprocal(rec[:, a:a + 2], den[:, a:a + 2]).then_inc(rec_ready, 1)
                dve.wait_ge(rec_ready, 2 * i + half + 1)
                for qt in HALVES[half]:
                    s = probs[:, P_BASE[qt]:P_BASE[qt] + P * key_tiles(i, qt)[1]]
                    dve.tensor_scalar(s, s, rec[:, qt:qt + 1], None, ALU.mult).then_inc(probs_ready, 1)

            def probs_t_lo(i, qt):
                n = order(i, qt)
                k0, nk = key_tiles(i, qt)
                dve.wait_ge(pt_hi_ready, n + 1)
                dve.tensor_tensor(pt_lo[:, k0:k0 + nk, P * qt:P * qt + P],
                                  bank[6 - n % 2][:, 0:P * nk].rearrange("p (k q) -> p k q", k=nk),
                                  pt_hi[:, k0:k0 + nk, P * qt:P * qt + P].bitcast(F32),
                                  ALU.subtract).then_inc(pt_lo_ready, 1)

            def gate_scale(j):
                dve.wait_ge(slab_done, G_GATE + j + 1)
                dve.tensor_tensor(store[:, j, :], bank[j % 2][:, :], r_all[:, :],
                                  ALU.mult).then_inc(acc_read, 1)

            scores_max(0, 0)
            normalise(0, 0)
            qkv_lo(N_QKV - 1)
            scores_max(0, 1)
            normalise(0, 1)
            gate_scale(0)
            for i in range(NH):
                probs_t_lo(i, 3)
                probs_t_lo(i, 2)
                if i + 1 < NH:
                    scores_max(i + 1, 0)
                probs_t_lo(i, 1)
                probs_t_lo(i, 0)
                if i + 1 < NH:
                    normalise(i + 1, 0)
                    scores_max(i + 1, 1)
                    normalise(i + 1, 1)
                    gate_scale(i + 1)
                if i % 2:
                    t = (Y_B + i // 2) if i < 8 else (Y_A + i // 2 - 4)
                    dve.wait_ge(y_hi_ready, i // 2 + 1)
                    dve.tensor_tensor(qk_lo[:, t, :], bank[7][:, :], qk_hi[:, t, :].bitcast(F32),
                                      ALU.subtract).then_inc(y_lo_ready, 1)

            for n in range(N_BRANCH):
                g = G_BRANCH + n
                dve.wait_ge(slab_done, g + 1)
                dve.wait_ge(gate_ready, 2 * n + 2)
                if n:
                    dve.wait_ge(m_lo_ready, n)
                dve.tensor_tensor(tmp_a, bank[2 * (n % 2) + 1][:, :], store[:, n, :],
                                  ALU.mult).then_inc(part_ready, 1)
                dve.tensor_tensor(tmp_b, bank[2 * (n % 2)][:, :], store[:, 8 + n, :],
                                  ALU.mult).then_inc(acc_read, 1)
                dve.wait_ge(part_ready, n + 1)
                dve.wait_ge(acc_read, read(g))
                dve.tensor_tensor(tmp_a, tmp_a, tmp_b, ALU.add).then_inc(m_ready, 1)
                dve.wait_ge(m_hi_ready, n + 1)
                dve.tensor_tensor(x_lo[:, n, :], tmp_a, x_hi[:, n, :].bitcast(F32),
                                  ALU.subtract).then_inc(m_lo_ready, 1)

            for n in range(N_OUT):
                g = G_OUT + n
                dve.wait_ge(slab_done, g + 1)
                dve.wait_ge(x2_arrived[n], 16)
                dve.tensor_tensor(store[:, n, :], bank[4 + n % 2][:, :], store[:, n, :],
                                  ALU.add).then_inc(acc_read, 1)
                dve.memset(store[:, 8 + n, :], 0.0)
                dve.wait_ge(x1_hi_ready, n + 1)
                dve.scalar_tensor_tensor(out=qk_lo[:, n, :], in0=store[:, n, :],
                                         scalar=par[:, C_FFN + n:C_FFN + n + 1],
                                         in1=qk_hi[:, n, :].bitcast(F32), op0=ALU.mult,
                                         op1=ALU.subtract).then_inc(x1_lo_ready, 1)
                if n:
                    dve.wait_ge(x1sq_ready, n + 1)
                    if n > 1:
                        dve.wait_ge(x1sum_ready, n - 1)
                    dve.tensor_tensor(r_all[:, :], r_all[:, :], (tmp_a, tmp_b)[n % 2],
                                      ALU.add).then_inc(x1sum_ready, 1)

            def up(j, c):
                g = G_FF + j
                dve.wait_ge(relu_ready, c * 8 + (j + 1))
                if j:
                    dve.wait_ge(u_lo_ready, c * 8 + j)
                dve.tensor_tensor(tmp_b, tmp_a, tmp_a, ALU.mult).then_inc(acc_read, 1)
                dve.wait_ge(u_hi_ready, c * 8 + (j + 1))
                dve.tensor_tensor(x_lo[:, j, :], tmp_b, x_hi[:, j, :].bitcast(F32),
                                  ALU.subtract).then_inc(u_lo_ready, 1)

            with dve.Fori(0, CHUNKS - 1) as c:
                for j in range(8):
                    up(j, c)
                for n in range(8):
                    g = G_FF + 8 + n
                    dve.wait_ge(slab_done, c * PER_CHUNK + (g + 1))
                    dve.tensor_tensor(store[:, 8 + n, :], bank[g % 2][:, :], store[:, 8 + n, :],
                                      ALU.add).then_inc(acc_read, 1)
            dve.wait_ge(ms2_done, 1)
            dve.tensor_scalar(ms_tok[:, :], bank[6][:, 0:QT], EPS, None, ALU.add).then_inc(ms2_ready, 1)
            dve.wait_ge(ms2_ready, 1)
            dve.reciprocal(r_tok[:, :], ms_tok[:, :]).then_inc(r2_ready, 1)
            for j in range(8):
                up(j, CHUNKS - 1)
            for n in range(8):
                g = N_SLABS - 8 + n
                o = store[:, 8 + n, :]
                dve.wait_ge(slab_done, g + 1)
                dve.tensor_tensor(o, bank[g % 2][:, :], o, ALU.add).then_inc(acc_read, 1)
                dve.wait_ge(acc_read, read(g))
                dve.wait_ge(r2_all_ready, 1)
                dve.tensor_tensor(o, o, r_all[:, :], ALU.mult).then_inc(scaled_ready, 1)
                dve.wait_ge(scaled_ready, n + 1)
                dve.tensor_tensor(o, o, store[:, n, :], ALU.add).then_inc(out_ready, 1)

        @block.tensor
        def _(pe):
            def products(out_, pairs, start, stop):
                last = None
                for a, (wh, wl, xh, xl) in enumerate(pairs):
                    first, end = start and a == 0, stop and a == len(pairs) - 1
                    pe.matmul(out_, wh, xh, start=first, stop=False)
                    pe.matmul(out_, wh, xl, start=False, stop=False)
                    last = pe.matmul(out_, wl, xh, start=False, stop=end)
                return last

            def weight(g, kt):
                c = slice(P * kt, P * kt + P)
                return w_hi[:, g % WS, c], w_lo[:, g % WS, c]

            def slab_part(g, acc, moving, kts, start=True, stop=True):
                return products(acc[:, :], [weight(g, kt) + moving(kt) for kt in kts], start, stop)

            def from_x(kt):
                return x_hi[:, kt, :], x_lo[:, kt, :]

            def from_qk(kt):
                return qk_hi[:, kt, :], qk_lo[:, kt, :]

            def spread(out_, by_token):
                for t in range(QT):
                    last = pe.transpose(out_[:, P * t:P * t + P], by_token(t), ident[:, :])
                return last

            def head_norm_sum(g):
                n = qk_count(g)
                pe.wait_ge(sq_ready, n + 1)
                if n >= 2:
                    pe.wait_ge(spread_ready, n - 1)
                for t in range(QT):
                    last = pe.matmul(bank[3 + n % 2][:, 2 * t:2 * t + 2], sq[:, P * t:P * t + P],
                                     head_cols[:, :], start=True, stop=True)
                last.then_inc(ss_done, 1)

            def head_norm_spread(g):
                if QKV_KIND[g] != "v":
                    n = qk_count(g)
                    pe.wait_ge(inv_ready, n + 1)
                    spread(bank[3 + n % 2], lambda t: inv_tok[:, P * t:P * t + P]).then_inc(spread_done, 1)

            def v_transpose(g):
                pe.wait_ge(pre_v_ready, v_count(g) + 1)
                if v_count(g):
                    pe.wait_ge(v_lo_ready, v_count(g))
                for t in range(QT):
                    last = pe.transpose(bank[5][:, P * t:P * t + P], pre_v[:, P * t:P * t + P], ident[:, :])
                last.then_inc(vt_done, 1)

            def after(g):
                if QKV_KIND[g] == "v":
                    v_transpose(g)
                else:
                    head_norm_sum(g)

            def qkv_read(g):
                if QKV_KIND[g] == "v":
                    pe.wait_ge(pre_v_ready, v_count(g) + 1)
                else:
                    pe.wait_ge(pre_ready, qk_count(g) + 1)

            def mean_square(total, out_):
                for t in range(QT):
                    last = pe.matmul(out_[:, t:t + 1], total[:, P * t:P * t + P], ones[:, :], start=True, stop=True)
                return last

            pe.wait_ge(const_ready, 4)
            pe.wait_ge(ident_ready, 2)
            for g in range(N_QKV):
                if g:
                    pe.wait_ge(w_lo_ready, g)
                if g >= 3:
                    qkv_read(g - 3)
                for kt in range(KT):
                    if g == 0:
                        pe.wait_ge(w0_lo_ready, 1 + kt // (KT // 2))
                        pe.wait_ge(x_lo_ready, kt + 1)
                    last = slab_part(g, bank[g % 3], from_x, [kt], kt == 0, kt == KT - 1)
                    if g >= 2 and kt == 1:
                        head_norm_spread(g - 2)
                    if g == 1 and kt == 6:
                        pe.wait_ge(xsum_ready, KT - 1)
                        mean_square(x_sum, bank[6]).then_inc(ms_done, 1)
                        after(0)
                    if g == 2 and kt == 6:
                        pe.wait_ge(r_sqrt, 1)
                        spread(bank[6], lambda t: r_tok[:, t:t + 1].to_broadcast([P, P])).then_inc(r_spread, 1)
                    if g == 4 and kt == 6:
                        pe.wait_ge(tab_arrived, 32)
                        pe.wait_ge(r_ready, 1)
                        pe.matmul(bank[7][0:NH, :], tabw, hot[:, 0:S], start=True, stop=True)
                        pe.matmul(bank[6][0:NH, :], tabw, hot[:, S:N_TAB], start=True,
                                  stop=True).then_inc(tab_done, 1)
                    if g >= 2 and kt == (3 if QKV_KIND[g - 1] != "v" else 5):
                        after(g - 1)
                last.then_inc(slab_done, 1)

            def scores(i, qt):
                n = order(i, qt)
                rows = slice(HD * (i % 2), HD * (i % 2) + HD)
                q = (1 + i // 2) if i < 8 else (Y_A + i // 2 - 4)
                k = 0 if i < 8 else 5 + i // 2 - 4
                k0, nk = key_tiles(i, qt)
                qs, ks = slice(P * qt, P * qt + P), slice(P * k0, P * (k0 + nk))
                if n >= 3:
                    pe.wait_ge(max_ready, n - 2)
                last = products(bank[2 + (n + 1) % 3][:, 0:P * nk],
                                [(qk_hi[rows, q, qs], qk_lo[rows, q, qs], qk_hi[rows, k, ks], qk_lo[rows, k, ks])],
                                True, True)
                last.then_inc(scores_done, 1)

            def probs_transpose(i, qt):
                n = order(i, qt)
                pe.wait_ge(probs_ready, n + 1)
                if n >= 2:
                    pe.wait_ge(pt_lo_ready, n - 1)
                for j in range(key_tiles(i, qt)[1]):
                    at = P_BASE[qt] + P * j
                    last = pe.transpose(bank[6 - n % 2][:, P * j:P * j + P], probs[:, at:at + P], ident[:, :])
                last.then_inc(pt_done, 1)

            def values(i):
                pe.wait_ge(pt_lo_ready, QT * (i + 1))
                if i % 2 == 0 and i:
                    pe.wait_ge(y_lo_ready, i // 2)
                v = 0 if i < 8 else 1 + i // 2 - 4
                e = i % 2
                for kt in reversed(range(QT)):
                    q0 = P * (QT - 1 - kt)
                    q1 = min(S, q0 + 2 * P) if i < 8 else S
                    vh, vl = v_hi[:, v, kt, e:e + 2, :], v_lo[:, v, kt, e:e + 2, :]
                    vh, vl = vh.rearrange("p a d -> p (a d)"), vl.rearrange("p a d -> p (a d)")
                    ph, pl = pt_hi[:, kt, q0:q1], pt_lo[:, kt, q0:q1]
                    o = bank[7][:, q0:q1]
                    for w, m in ((vh, ph), (vh, pl), (vl, ph)):
                        last = pe.matmul(o, w, m, start=(e == 0 and kt == QT - 1 and w is vh and m is ph),
                                         stop=(e == 1 and kt == 0 and w is vl), skip_group_check=True)
                last.then_inc(pv_done, 1)

            def gate_part(j, kts, stop):
                g = G_GATE + j
                if kts[0] == 0:
                    pe.wait_ge(w_lo_ready, g)
                    if j < 2:
                        qkv_read(g - 3)
                    else:
                        pe.wait_ge(acc_read, read(g - 2))
                last = slab_part(g, bank[j % 2], from_x, kts, kts[0] == 0, stop)
                if stop:
                    last.then_inc(slab_done, 1)

            pe.wait_ge(qk_lo_ready, N_QK)
            scores(0, 3)
            scores(0, 2)
            gate_part(0, [0, 1, 2], False)
            pe.wait_ge(pre_v_ready, N_V)
            scores(0, 1)
            scores(0, 0)
            after(N_QKV - 1)
            gate_part(0, [3, 4, 5, 6, 7], True)
            for i in range(NH - 1):
                probs_transpose(i, 3)
                if i == 0:
                    pe.wait_ge(v_lo_ready, N_V)
                probs_transpose(i, 2)
                scores(i + 1, 3)
                scores(i + 1, 2)
                gate_part(i + 1, [0, 1, 2], False)
                probs_transpose(i, 1)
                probs_transpose(i, 0)
                scores(i + 1, 1)
                scores(i + 1, 0)
                gate_part(i + 1, [3, 4, 5, 6, 7], True)
                values(i)

            def branch_b(n):
                g = G_BRANCH + n
                pe.wait_ge(w_lo_ready, g)
                if n == 0:
                    pe.wait_ge(acc_read, read(G_BRANCH - 1))
                elif n == 1:
                    pe.wait_ge(max_ready, QT * NH)
                else:
                    pe.wait_ge(acc_read, read(g - 2))
                slab_part(g, bank[2 * (n % 2)], lambda kt: from_qk(Y_B + kt), [0, 1, 2, 3])

            def branch_a(n, kts):
                last = slab_part(G_BRANCH + n, bank[2 * (n % 2) + 1], lambda kt: from_qk(Y_A + kt - 4), kts,
                                 kts[0] == 4, kts[-1] == 7)
                if kts[-1] == 7:
                    last.then_inc(slab_done, 1)

            probs_transpose(NH - 1, 3)
            probs_transpose(NH - 1, 2)
            branch_b(0)
            probs_transpose(NH - 1, 1)
            probs_transpose(NH - 1, 0)
            pe.wait_ge(y_lo_ready, 7)
            branch_a(0, [4, 5, 6])
            values(NH - 1)
            branch_b(1)
            pe.wait_ge(y_lo_ready, 8)
            branch_a(0, [7])
            branch_a(1, [4, 5, 6, 7])
            for n in range(2, N_BRANCH):
                branch_b(n)
                branch_a(n, [4, 5, 6, 7])

            for n in range(N_OUT):
                g = G_OUT + n
                pe.wait_ge(w_lo_ready, g)
                if n >= 2:
                    pe.wait_ge(acc_read, read(g - 2))
                for kt in range(KT):
                    if n == 0:
                        pe.wait_ge(m_lo_ready, kt + 1)
                    last = slab_part(g, bank[4 + n % 2], from_x, [kt], kt == 0, kt == KT - 1)
                last.then_inc(slab_done, 1)

            def feed_forward(c, last_chunk=False):
                at = c * PER_CHUNK
                for j in range(8):
                    g = G_FF + j
                    pe.wait_ge(w_lo_ready, at + g)
                    pe.wait_ge(acc_read, at + read(g - 2))
                    for kt in range(KT):
                        if j == 0:
                            pe.wait_ge(x1_lo_ready, kt + 1)
                        last = slab_part(g, bank[g % 2], from_qk, [kt], kt == 0, kt == KT - 1)
                    last.then_inc(slab_done, 1)
                    if last_chunk and j == 1:
                        pe.wait_ge(r2_ready, 1)
                        spread(bank[7], lambda t: r_tok[:, t:t + 1].to_broadcast([P, P])).then_inc(r2_spread, 1)
                for n in range(8):
                    g = G_FF + 8 + n
                    pe.wait_ge(w_lo_ready, at + g)
                    pe.wait_ge(acc_read, at + read(g - 2))
                    for kt in range(KT):
                        if n == 0:
                            pe.wait_ge(u_lo_ready, c * 8 + (kt + 1))
                        last = slab_part(g, bank[g % 2], from_x, [kt], kt == 0, kt == KT - 1)
                    last.then_inc(slab_done, 1)

            with pe.Fori(0, CHUNKS - 1) as c:
                feed_forward(c)
            pe.wait_ge(x1sum_ready, N_OUT - 1)
            mean_square(r_all, bank[6]).then_inc(ms2_done, 1)
            feed_forward(CHUNKS - 1, True)


def rel_bucket(n):
    n = np.maximum(n, 0)
    exact = NBUCKET // 2
    nf = np.maximum(n, 1).astype(np.float32)
    large = exact + (np.log(nf / np.float32(exact)) / np.float32(np.log(MAXDIST / exact))
                     * np.float32(NBUCKET - exact)).astype(np.int32)
    return np.where(n < exact, n, np.minimum(large, NBUCKET - 1))


def distance_onehot():
    hot = np.zeros((NBUCKET + 1, N_TAB), np.float32)
    for at, n, limit in ((T_A, T_B, S), (T_B, N_TAB - T_B, WINDOW)):
        d = np.arange(n) - (P - 1)
        row = np.where((d >= 0) & (d < limit), rel_bucket(d), NBUCKET)
        hot[row, at + np.arange(n)] = 1.0
    return hot


def as_slabs(w):
    n = w.shape[1] // P
    return w.reshape(KT, P, n, P).transpose(2, 1, 0, 3).reshape(n, P, D)


def kernel(**inputs):
    import concourse.bacc as bacc
    from concourse.bass_utils import run_bass_kernel_spmd

    a = {k: np.asarray(v) for k, v in inputs.items()}
    order_b = [t + 4 * e for t in range(4) for e in range(2)]
    w_in = a["w_in"][0]
    wa = 8 * HD
    at = np.cumsum([0, wa, wa, wa, wa, 2 * HD, 2 * HD, D])
    qa, ka, va, qb, kb, vb, ga, gb = (w_in[:, i:j] for i, j in zip(at, [*at[1:], w_in.shape[1]]))
    qb = qb.reshape(D, 8, HD)[:, order_b].reshape(D, wa)
    ka, qa = ka.reshape(D, 4, P), qa.reshape(D, 4, P)
    kq = [t[:, p] for p in range(4) for t in (ka, qa)]
    w_qkv = np.concatenate([kb, qb, vb, *kq, va, ga, gb], axis=1)
    branch_b = a["w_branch_b"][0].reshape(8, HD, D)[order_b].reshape(wa, D)
    w_branch = np.concatenate([branch_b, a["w_branch_a"][0]], axis=0)
    ff1 = as_slabs(a["w_ff1"][0]).reshape(CHUNKS, 8, P, D)
    ff2 = np.stack([as_slabs(w) for w in a["w_ff2"][0].reshape(CHUNKS, D, D)])
    slabs = np.concatenate([as_slabs(w_qkv), as_slabs(w_branch), as_slabs(a["w_out"][0]),
                            np.concatenate([ff1, ff2], axis=1).reshape(CHUNKS * PER_CHUNK, P, D)])

    def columns(v):
        return v.reshape(-1, P).T

    def twice(v):
        return np.tile(v.reshape(-1, 1), (2, 1))

    params = np.concatenate(
        [columns(a["g_mix"]), columns(a["g_ffn"]), columns(a["b_gate"]), twice(a["k_norm_b"]),
         twice(a["q_norm_b"]), twice(a["k_norm_a"]), twice(a["q_norm_a"]),
         np.tile(a["sinks"].reshape(1, 8)[:, order_b], (P, 1))], axis=1)
    table = np.concatenate([a["rel_bias"][:, 8:][:, order_b], a["rel_bias"][:, :8]], axis=1)
    arrays = {
        "x_t": a["x"].reshape(S, D).T.reshape(KT, P, S),
        "slabs": slabs, "params": params, "table": table, "onehot": distance_onehot(),
    }
    arrays = {k: np.ascontiguousarray(v) for k, v in arrays.items()}
    nc = bacc.Bacc("TRN2", target_bir_lowering=False, num_devices=1)
    F32 = mybir.dt.float32
    aps = [nc.dram_tensor(k, v.shape, F32, kind="ExternalInput").ap() for k, v in arrays.items()]
    tab_dram = nc.dram_tensor("tab_dram", (NH, N_TAB), F32, kind="Internal").ap()
    out = nc.dram_tensor("out", (KT, P, S), F32, kind="ExternalOutput").ap()
    build(nc, *aps, tab_dram, out)
    r = run_bass_kernel_spmd(nc, [arrays], core_ids=[0])
    return r.results[0]["out"].reshape(D, S).T.reshape(1, S, D)
```

```python
import numpy as np
import concourse.bass as bass
from concourse import mybir
from contextlib import ExitStack

D, S, HD, DFF = 1024, 512, 64, 4096
P = 128
KT = D // P
QT = S // P
NBUCKET, MAXDIST, WINDOW = 32, 2048, 128
EPS = 1e-6
MASK = -1e30
NH = 16

KV_B, V_B = 0, 5
N_QKV, N_GATE, N_BRANCH, N_OUT = 18, 16, 8, 8
G_GATE = N_QKV
G_BRANCH = G_GATE + N_GATE
G_OUT = G_BRANCH + N_BRANCH
G_FF = G_OUT + N_OUT
CHUNKS = 4
PER_CHUNK = 16
N_SLABS = G_FF + CHUNKS * PER_CHUNK
LATE = G_BRANCH + 2
LOOP_FROM = LATE + 2
RAW, WS = 4, 2
FIRST = 2
N_REST = KT // FIRST - 1
WARM_UP = 10

QKV_KIND = ["k", "q", "q", "q", "q", "v"] + ["k", "q"] * 4 + ["v"] * 4
QKV_TILE = [0, 1, 2, 3, 4, 0] + [5, 9, 6, 10, 7, 11, 8, 12] + [1, 2, 3, 4]
K_SLAB = {t: g for g, t in enumerate(QKV_TILE) if QKV_KIND[g] == "k"}
Y_B, Y_A = 1, 9
C_MIX, C_FFN, C_BGATE, C_NORM, C_SINK, N_PAR = 0, 8, 16, 32, 36, 44
T_A, T_B, N_TAB = 0, 640, 1024
P_BASE = [0, 128, 384, 768]


def norm_column(slab):
    return C_NORM + (0 if slab < V_B else 2) + (QKV_KIND[slab] == "q")


def build(nc, x_t, slabs, params, table, onehot, tab_dram, out):
    F32, R = mybir.dt.float32, mybir.dt.float32r
    ALU, ACT = mybir.AluOpType, mybir.ActivationFunctionType
    ctx = ExitStack()
    with ctx:
        def sb(name, shape, dt):
            return ctx.enter_context(nc.sbuf_tensor(name, shape, dt))

        def sem(name):
            return ctx.enter_context(nc.semaphore(name))

        w_raw = sb("w_raw", [P, RAW, D], F32)
        w_hi, w_lo = sb("w_hi", [P, WS, D], R), sb("w_lo", [P, WS, D], R)
        x_hi, x_lo = sb("x_hi", [P, KT, S], R), sb("x_lo", [P, KT, S], R)
        qk_hi, qk_lo = sb("qk_hi", [P, 13, S], R), sb("qk_lo", [P, 13, S], R)
        even, odd = qk_hi, qk_lo
        k_lo = sb("k_lo", [P, 5, S], R)
        v_parts = sb("v_parts", [P, 5, QT, 4, HD], R)
        store = sb("store", [P, 16, S], F32)
        pt_hi, pt_lo = sb("pt_hi", [P, QT, S], R), sb("pt_lo", [P, QT, S], R)
        y_both = sb("y_both", [P, S], F32)
        probs = sb("probs", [P, 1280], F32)
        bias_m = sb("bias_m", [P, 2, S], F32)
        r_all = sb("r_all", [P, S], F32)
        ident = sb("ident", [P, P], F32)
        ones = sb("ones", [P, 1], F32)
        head_ones = pt_lo[:, 1, 0:P]
        par = sb("par", [P, N_PAR], F32)
        softmax = sb("softmax", [P, 5, QT], F32)
        top, neg, den, sink_e, rec = (softmax[:, j, :] for j in range(5))
        bank = [ctx.enter_context(nc.psum_tensor(f"bank{i}", [P, 512], F32)) for i in range(8)]

        xsq = [store[:, j, :] for j in (8, 9, 10, 11)]
        x_sum = store[:, 12, :]
        r_inv_sq = store[:, 11, :]
        r_root, r_root_sq = store[:, 6, :], store[:, 10, :]
        sq, mean_sq, root, root_sq, fix = (store[:, j, :] for j in (14, 15, 8, 7, 9))
        pre = [store[:, 13, :], store[:, 5, :]]
        sq_hi, sq_lo = pt_hi[:, 0, :], pt_lo[:, 0, :]
        pre_v = store[:, 10, :]
        tab = bias_m[0:NH, :, :].rearrange("p a n -> p (a n)")
        hot = probs[0:NBUCKET + 1, 0:N_TAB]
        tabw = probs[0:NBUCKET + 1, N_TAB:N_TAB + NH]
        tmp_a, tmp_b = probs[:, 0:S], probs[:, S:2 * S]

        arrived = [sem(f"slab_arrived{i}") for i in range(RAW)]
        x_arrived = [sem(f"x_arrived{i}") for i in range(KT)]
        par_arrived = sem("par_arrived")
        tab_arrived = sem("tab_arrived")
        tab_stored = sem("tab_stored")
        bias_arrived = [sem("bias_arrived0"), sem("bias_arrived1")]
        out_stored = sem("out_stored")
        const_ready, ident_ready = sem("const_ready"), sem("ident_ready")
        par_ready = sem("par_ready")
        w_hi_ready, w_lo_ready = sem("w_hi_ready"), sem("w_lo_ready")
        slab_done = sem("slab_done")
        acc_read = sem("acc_read")
        x_hi_ready, x_lo_ready = sem("x_hi_ready"), sem("x_lo_ready")
        xsq_ready, xsum_ready = sem("xsq_ready"), sem("xsum_ready")
        first_arrived = [sem("first_arrived0"), sem("first_arrived1")]
        first_ready = sem("first_ready")
        rest_ready = sem("rest_ready")
        ms_done, ms_ready, r_root_ready, r_ready = (sem(n) for n in ("ms_done", "ms_ready", "r_root_ready", "r_ready"))
        tab_done, tab_copied = sem("tab_done"), sem("tab_copied")
        pre_ready, pre_v_ready = sem("pre_ready"), sem("pre_v_ready")
        sq_ready, ss_done, ss_read = sem("sq_ready"), sem("ss_done"), sem("ss_read")
        sq_lo_ready = sem("sq_lo_ready")
        root_ready, fix_ready = sem("root_ready"), sem("fix_ready")
        qk_hi_ready, qk_lo_ready = sem("qk_hi_ready"), sem("qk_lo_ready")
        even_lo_ready, k_twice_ready = sem("even_lo_ready"), sem("k_twice_ready")
        vt_done, v_hi_ready, v_lo_ready = sem("vt_done"), sem("v_hi_ready"), sem("v_lo_ready")
        scores_done, max_ready, neg_ready = sem("scores_done"), sem("max_ready"), sem("neg_ready")
        exp_ready, sink_ready = sem("exp_ready"), sem("sink_ready")
        den_ready, rec_ready, probs_ready = sem("den_ready"), sem("rec_ready"), sem("probs_ready")
        pt_done, pt_hi_ready, pt_lo_ready = sem("pt_done"), sem("pt_hi_ready"), sem("pt_lo_ready")
        pv_done, y_part_ready, y_sum_ready = sem("pv_done"), sem("y_part_ready"), sem("y_sum_ready")
        y_hi_ready, y_lo_ready = sem("y_hi_ready"), sem("y_lo_ready")
        gate_ready = sem("gate_ready")
        part_ready, m_ready = sem("part_ready"), sem("m_ready")
        m_hi_ready, m_lo_ready = sem("m_hi_ready"), sem("m_lo_ready")
        x2_arrived = [sem(f"x2_arrived{i}") for i in range(KT)]
        x1_hi_ready, x1_lo_ready = sem("x1_hi_ready"), sem("x1_lo_ready")
        x1sq_ready, x1sum_ready = sem("x1sq_ready"), sem("x1sum_ready")
        ms2_done, ms2_ready, r2_ready = sem("ms2_done"), sem("ms2_ready"), sem("r2_ready")
        relu_ready, u_hi_ready, u_lo_ready = sem("relu_ready"), sem("u_hi_ready"), sem("u_lo_ready")
        scaled_ready, rest_sum_ready = sem("scaled_ready"), sem("rest_sum_ready")
        out_ready = sem("out_ready")
        half_done = sem("half_done")

        def qk_count(slab):
            return sum(kind != "v" for kind in QKV_KIND[:slab])

        def v_count(slab):
            return sum(kind == "v" for kind in QKV_KIND[:slab])

        def read(g):
            return g - N_QKV + 1

        def acc(g):
            return bank[{3: 5, 4: 6, 5: 7}.get(g, g % 3)]

        N_QK, N_V = qk_count(N_QKV), v_count(N_QKV)

        def key_tiles(i, qt):
            return QT - 1 - qt, min(2, qt + 1) if i < 8 else qt + 1

        def order(i, qt):
            return QT * i + (QT - 1 - qt)

        HALVES = [(3, 2), (1, 0)]

        EVEN, ODD = slice(0, HD), slice(HD, P)

        def k_tile(t):
            return t - 4 if t else 0

        def y_tile(i):
            return (Y_B + i // 2) if i < 8 else (Y_A + i // 2 - 4)

        def branch_banks(n):
            return (bank[2], bank[1]) if n % 2 else (bank[0], bank[3])

        def y_part(i):
            return store[0:HD, 15, :] if i < NH - 2 else bias_m[0:HD, 0, :]

        def y_rows(i):
            return slice(HD * (i % 2), HD * (i % 2) + HD)

        HALF_TOKENS = [slice(0, S // 2), slice(S // 2, S)]

        block = ctx.enter_context(nc.Block())

        @block.sync
        def _(sp):
            def load_slab(g):
                if g >= RAW:
                    if g < RAW + 2:
                        sp.wait_ge(first_ready, g - RAW + 1)
                    if g > RAW:
                        sp.wait_ge(w_lo_ready, g - RAW)
                    else:
                        sp.wait_ge(rest_ready, N_REST)
                sp.dma_start(w_raw[:, g % RAW, :], slabs[g]).then_inc(arrived[g % RAW], 16)

            def load_first(g):
                sp.dma_start(w_raw[:, g, 0:FIRST * P], slabs[g][:, 0:FIRST * P]).then_inc(first_arrived[g], 16)

            def load_rest(g):
                sp.dma_start(w_raw[:, g, FIRST * P:D], slabs[g][:, FIRST * P:D]).then_inc(arrived[g], 16)

            def load_bias(i):
                if i >= 2:
                    sp.wait_ge(max_ready, QT * (i - 1))
                else:
                    sp.wait_ge(tab_stored, 16)
                at, n = (T_B, 2 * P) if i < 8 else (T_A, S)
                src = bass.AP(tensor=tab_dram.tensor, offset=i * N_TAB + at, ap=[[1, P], [1, n]])
                sp.dma_start(bias_m[:, i % 2, 0:n], src).then_inc(bias_arrived[i % 2], 16)

            sp.dma_start(par[:, :], params).then_inc(par_arrived, 16)
            for k in range(KT):
                sp.dma_start(store[:, k, :], x_t[k]).then_inc(x_arrived[k], 16)
                if k == 0:
                    load_first(0)
                if k == 1:
                    load_rest(0)
            load_first(1)
            load_rest(1)
            sp.dma_start(hot, onehot).then_inc(tab_arrived, 16)
            sp.dma_start(tabw[0:NBUCKET, :], table).then_inc(tab_arrived, 16)
            for g in range(2, G_FF):
                if g == 14:
                    sp.wait_ge(tab_copied, 2)
                    sp.dma_start(tab_dram, tab).then_inc(tab_stored, 16)
                if g == 16:
                    load_bias(0)
                    load_bias(1)
                if 2 <= g - 22 < NH:
                    load_bias(g - 22)
                if G_BRANCH + 6 <= g < G_OUT + 6:
                    n = g - G_BRANCH - 6
                    sp.wait_ge(acc_read, read(G_BRANCH + n))
                    sp.dma_start(store[:, n, :], x_t[n]).then_inc(x2_arrived[n], 16)
                load_slab(g)
            with sp.Fori(0, CHUNKS) as c:
                for k in range(PER_CHUNK):
                    g = sp.snap(c * PER_CHUNK + (G_FF + k))
                    sp.wait_ge(w_lo_ready, c * PER_CHUNK + (G_FF + k - RAW))
                    sp.dma_start(w_raw[:, (G_FF + k) % RAW, :],
                                 slabs[bass.ds(g, 1)].rearrange("a p n -> (a p) n")
                                 ).then_inc(arrived[(G_FF + k) % RAW], 16)
            for n in range(KT - 1):
                sp.wait_ge(out_ready, n + 1)
                sp.dma_start(out[n], store[:, 8 + n, :]).then_inc(out_stored, 16)
            for h, part in enumerate(HALF_TOKENS):
                sp.wait_ge(out_ready, KT + h)
                sp.dma_start(out[KT - 1][:, part], store[:, 8 + KT - 1, part]).then_inc(out_stored, 16)
            sp.wait_ge(out_stored, 16 * (KT + 1))

        @block.gpsimd
        def _(pool):
            pool.memset(ident[:, :], 0.0).then_inc(ident_ready, 1)
            pool.wait_ge(ident_ready, 1)
            pool.affine_select(out=ident[:, :], in_=ident[:, :], compare_op=ALU.not_equal, fill=1.0,
                               base=0, pattern=[[-1, P]], channel_multiplier=1).then_inc(ident_ready, 1)

            def split_lo(g, count):
                pool.wait_ge(w_hi_ready, count)
                pool.tensor_tensor(w_lo[:, g % WS, :], w_raw[:, g % RAW, :],
                                   w_hi[:, g % WS, :].bitcast(F32), ALU.subtract).then_inc(w_lo_ready, 1)

            for g in range(2):
                pool.wait_ge(w_hi_ready, 2 * g + 2)
                for k in range(FIRST, KT, FIRST):
                    part = slice(P * k, P * (k + FIRST))
                    pool.tensor_tensor(w_lo[:, g, part], w_raw[:, g, part], w_hi[:, g, part].bitcast(F32),
                                       ALU.subtract).then_inc(w_lo_ready if g and k + FIRST == KT else rest_ready, 1)

            def qk_split_lo(g, s):
                t, n = QKV_TILE[g], qk_count(g)
                pool.wait_ge(qk_hi_ready, n + 1)
                pool.wait_ge(w_lo_ready, s)
                if QKV_KIND[g] == "q":
                    lo_even, lo_odd = even[ODD, t, :], odd[EVEN, t, :]
                else:
                    kt = k_tile(t)
                    lo_even, lo_odd = k_lo[EVEN, kt, :], k_lo[ODD, kt, :]
                pool.tensor_tensor(lo_even, pre[n % 2][EVEN, :], even[EVEN, t, :].bitcast(F32),
                                   ALU.subtract).then_inc(even_lo_ready, 1)
                pool.wait_ge(even_lo_ready, n + 1)
                pool.tensor_tensor(lo_odd, pre[n % 2][ODD, :], odd[ODD, t, :].bitcast(F32),
                                   ALU.subtract).then_inc(qk_lo_ready, 1)
                pool.wait_ge(qk_lo_ready, n + 1)

            for s in range(2, LOOP_FROM):
                if s != LATE:
                    split_lo(s, s + 3)
                g = s - 4 if s <= V_B + 3 else s - 3
                if 0 <= g < N_QKV and QKV_KIND[g] != "v":
                    qk_split_lo(g, s)
            with pool.Fori(0, (N_SLABS - LOOP_FROM) // RAW) as c:
                for k in range(RAW):
                    split_lo(LOOP_FROM + k, c * RAW + (LOOP_FROM + k + 3))

        @block.scalar
        def _(act):
            def split_hi(g, c=None):
                at = 0 if c is None else c * PER_CHUNK
                act.wait_ge(arrived[g % RAW], 16 * (g // RAW + 1) + (0 if c is None else c * (16 * PER_CHUNK // RAW)))
                if g >= WS:
                    act.wait_ge(slab_done, at + (g - WS + 1))
                act.activation(w_hi[:, g % WS, :], w_raw[:, g % RAW, :], ACT.Copy).then_inc(w_hi_ready, 1)

            def hi_part(g, part, loaded):
                act.wait_ge(loaded, 16)
                act.activation(w_hi[:, g, part], w_raw[:, g, part], ACT.Copy).then_inc(w_hi_ready, 1)

            act.preload_act_table_set("natural_log_exp_and_others")
            act.wait_ge(par_arrived, 16)
            for k in range(KT):
                if k == 1:
                    hi_part(0, slice(0, FIRST * P), first_arrived[0])
                if k == 2:
                    hi_part(0, slice(FIRST * P, D), arrived[0])
                act.wait_ge(x_arrived[k], 16)
                act.activation(x_hi[:, k, :], store[:, k, :], ACT.Copy,
                               scale=par[:, C_MIX + k:C_MIX + k + 1]).then_inc(x_hi_ready, 1)
            hi_part(1, slice(0, FIRST * P), first_arrived[1])
            hi_part(1, slice(FIRST * P, D), arrived[1])
            for k in range(KT):
                if k == 3:
                    split_hi(2)
                if k > 4:
                    act.wait_ge(xsum_ready, k - 4)
                act.activation(xsq[k % 4] if k else x_sum, store[:, k, :], ACT.Square).then_inc(xsq_ready, 1)

            def qkv_square(g):
                if QKV_KIND[g] != "v":
                    n = qk_count(g)
                    act.wait_ge(slab_done, g + 1)
                    if n:
                        act.wait_ge(sq_lo_ready, n)
                        act.wait_ge(ss_done, n)
                    act.activation(sq_hi, acc(g)[:, :], ACT.Square).then_inc(sq_ready, 1)
                    act.activation(sq, acc(g)[:, :], ACT.Square).then_inc(sq_ready, 1)

            def power(out_, square, in_, ready, count):
                act.activation(out_, in_, ACT.Ln).then_inc(ready, 1)
                act.wait_ge(ready, count - 2)
                act.activation(out_, out_, ACT.Exp, scale=-0.5).then_inc(ready, 1)
                act.wait_ge(ready, count - 1)
                act.activation(square, out_, ACT.Square).then_inc(ready, 1)

            def qkv_hi(g):
                t = QKV_TILE[g]
                if QKV_KIND[g] != "v":
                    act.wait_ge(pre_ready, qk_count(g) + 1)
                    n = qk_count(g) % 2
                    act.activation(even[EVEN, t, :], pre[n][EVEN, :], ACT.Copy)
                    act.activation(odd[ODD, t, :], pre[n][ODD, :], ACT.Copy).then_inc(qk_hi_ready, 1)
                else:
                    act.wait_ge(vt_done, v_count(g) + 1)
                    act.activation(v_parts[:, t, :, 0::2, :],
                                   bank[5][:, :].rearrange("p (t e d) -> p t e d", t=QT, e=2),
                                   ACT.Copy).then_inc(v_hi_ready, 1)

            def qkv_root(g):
                if QKV_KIND[g] != "v":
                    n = qk_count(g)
                    act.wait_ge(ss_read, n + 1)
                    if n:
                        act.wait_ge(fix_ready, 2 * n)
                    power(root, root_sq, mean_sq, root_ready, 3 * n + 3)

            for g in range(N_QKV):
                if g and QKV_KIND[g - 1] == "v":
                    qkv_hi(g - 1)
                if g == 1:
                    split_hi(3)
                if g == 2:
                    qkv_square(3)
                elif g not in (3, 4, 7):
                    qkv_square(g)
                if g in (2, 3, 5):
                    split_hi(g + 3)
                if g == 3:
                    qkv_square(4)
                if g > 6:
                    split_hi(g + 2)
                if g == 1:
                    qkv_root(0)
                    split_hi(4)
                    qkv_square(2)
                if g == 4:
                    act.wait_ge(ms_ready, 1)
                    power(r_root, r_root_sq, r_inv_sq, r_root_ready, 3)
                    split_hi(7)
                if g and QKV_KIND[g - 1] != "v":
                    qkv_hi(g - 1)
                if g == 6:
                    qkv_square(7)
                if g:
                    qkv_root(g)

            def exps(i, half):
                act.wait_ge(neg_ready, 2 * i + half + 1)
                for qt in HALVES[half]:
                    n = P * key_tiles(i, qt)[1]
                    s = probs[:, P_BASE[qt]:P_BASE[qt] + n]
                    act.activation(s, s, ACT.Exp, bias=neg[:, qt:qt + 1],
                                   accum_out=den[:, qt:qt + 1]).then_inc(exp_ready, 1)
                if i < 8:
                    a = HALVES[half][1]
                    act.activation(sink_e[:, a:a + 2], neg[:, a:a + 2], ACT.Exp,
                                   bias=par[:, C_SINK + i:C_SINK + i + 1]).then_inc(sink_ready, 1)

            def probs_t_hi(i, qt):
                n = order(i, qt)
                k0, nk = key_tiles(i, qt)
                act.wait_ge(pt_done, n + 1)
                act.activation(pt_hi[:, k0:k0 + nk, P * qt:P * qt + P],
                               bank[6 - n % 2][:, 0:P * nk].rearrange("p (k q) -> p k q", k=nk),
                               ACT.Copy).then_inc(pt_hi_ready, 1)

            def gate(n):
                for j in (n, 8 + n):
                    act.wait_ge(acc_read, read(G_GATE + j))
                    act.activation(store[:, j, :], store[:, j, :], ACT.Sigmoid,
                                   bias=par[:, C_BGATE + j:C_BGATE + j + 1]).then_inc(gate_ready, 1)

            def y_hi(i):
                act.wait_ge(y_sum_ready, i + 1)
                act.activation(qk_hi[:, y_tile(i), :], y_both[:, :], ACT.Copy).then_inc(y_hi_ready, 1)

            exps(0, 0)
            qkv_hi(N_QKV - 1)
            exps(0, 1)
            for i in range(NH):
                probs_t_hi(i, 3)
                probs_t_hi(i, 2)
                split_hi(G_GATE + 2 + i)
                if i + 1 < NH:
                    exps(i + 1, 0)
                probs_t_hi(i, 1)
                probs_t_hi(i, 0)
                if i and i % 2 == 0:
                    y_hi(i - 1)
                if i + 1 < NH:
                    exps(i + 1, 1)
                else:
                    act.preload_act_table(ACT.Sigmoid)
                    gate(0)
                act.wait_ge(pv_done, i + 1)
                act.activation(y_part(i), bank[7][HD:P, :], ACT.Copy).then_inc(y_part_ready, 1)
            y_hi(NH - 1)

            for n in range(N_BRANCH):
                split_hi(G_BRANCH + n + 2)
                if n + 1 < N_BRANCH:
                    gate(n + 1)
                act.wait_ge(m_ready, n + 1)
                act.activation(x_hi[:, n, :], tmp_a, ACT.Copy).then_inc(m_hi_ready, 1)

            for n in range(N_OUT):
                act.wait_ge(acc_read, read(G_OUT + n))
                act.activation(qk_hi[:, n, :], store[:, n, :], ACT.Copy,
                               scale=par[:, C_FFN + n:C_FFN + n + 1]).then_inc(x1_hi_ready, 1)
                split_hi(G_OUT + n + 2)
                if n >= 3:
                    act.wait_ge(x1sum_ready, n - 2)
                act.activation((tmp_a, tmp_b)[n % 2] if n else r_all[:, :], store[:, n, :],
                               ACT.Square).then_inc(x1sq_ready, 1)

            def up(j, c, last=False):
                g = G_FF + j
                at = c * PER_CHUNK
                act.wait_ge(slab_done, at + (g + 1))
                act.activation(tmp_a, bank[g % 2][:, :], ACT.Relu).then_inc(relu_ready, 1)
                if isinstance(c, int):
                    split_hi(g + 2 + c * PER_CHUNK)
                else:
                    split_hi(g + 2, c)
                act.wait_ge(acc_read, at + read(g))
                act.activation(x_hi[:, j, :], tmp_b, ACT.Copy).then_inc(u_hi_ready, 1)

            act.wait_ge(x1sum_ready, N_OUT - 1)
            with act.Fori(0, CHUNKS - 1) as c:
                for j in range(8):
                    up(j, c)
                for n in range(8):
                    split_hi(G_FF + 8 + n + 2, c)
            for j in range(8):
                up(j, CHUNKS - 1)
            for n in range(6):
                split_hi(N_SLABS - 8 + n + 2)

        @block.vector
        def _(dve):
            dve.memset(ones[:, :], 1.0 / D).then_inc(const_ready, 1)
            for a in range(2):
                for b in range(2):
                    last = dve.memset(head_ones[HD * a:HD * (a + 1), HD * b:HD * (b + 1)].bitcast(F32),
                                      1.0 / HD if a == b else 0.0)
            last.then_inc(const_ready, 1)
            dve.memset(tabw[NBUCKET:NBUCKET + 1, :], MASK).then_inc(const_ready, 1)
            dve.wait_ge(par_arrived, 16)
            for a in (1, 3):
                col = par[:, C_NORM + a:C_NORM + a + 1]
                dve.tensor_scalar(col, col, HD ** -0.5, None, ALU.mult).then_inc(par_ready, 1)

            def split_first(g):
                part = slice(0, FIRST * P)
                dve.wait_ge(w_hi_ready, 2 * g + 1)
                dve.tensor_tensor(w_lo[:, g, part], w_raw[:, g, part], w_hi[:, g, part].bitcast(F32),
                                  ALU.subtract).then_inc(first_ready, 1)

            for k in range(KT):
                if k == 1:
                    split_first(0)
                dve.wait_ge(x_hi_ready, k + 1)
                dve.scalar_tensor_tensor(out=x_lo[:, k, :], in0=store[:, k, :],
                                         scalar=par[:, C_MIX + k:C_MIX + k + 1],
                                         in1=x_hi[:, k, :].bitcast(F32), op0=ALU.mult,
                                         op1=ALU.subtract).then_inc(x_lo_ready, 1)
            split_first(1)
            for k in range(1, KT):
                dve.wait_ge(xsq_ready, k + 1)
                if k > 1:
                    dve.wait_ge(xsum_ready, k - 1)
                dve.tensor_tensor(x_sum, x_sum, xsq[k % 4], ALU.add).then_inc(xsum_ready, 1)

            def refine(out_, root_, square, x, ready, count):
                dve.scalar_tensor_tensor(out=out_, in0=square, scalar=-0.5, in1=x, op0=ALU.mult,
                                         op1=ALU.mult).then_inc(ready, 1)
                dve.wait_ge(ready, count - 1)
                dve.scalar_tensor_tensor(out=out_, in0=out_, scalar=1.5, in1=root_, op0=ALU.add,
                                         op1=ALU.mult).then_inc(ready, 1)

            def qk_split_squares(g):
                if QKV_KIND[g] != "v":
                    n = qk_count(g)
                    dve.wait_ge(sq_ready, 2 * n + 2)
                    if n:
                        dve.wait_ge(ss_done, n)
                    dve.tensor_tensor(sq_lo, sq, sq_hi.bitcast(F32), ALU.subtract).then_inc(sq_lo_ready, 1)

            def qk_mean(g):
                if QKV_KIND[g] != "v":
                    n = qk_count(g)
                    dve.wait_ge(ss_done, n + 1)
                    if n == 0:
                        dve.wait_ge(ms_done, 1)
                        dve.tensor_scalar(r_inv_sq, bank[6][:, :], EPS, None, ALU.add).then_inc(ms_ready, 1)
                        dve.wait_ge(ms_ready, 1)
                    else:
                        dve.wait_ge(fix_ready, 2 * n)
                    dve.scalar_tensor_tensor(out=mean_sq, in0=r_inv_sq, scalar=EPS, in1=bank[3 + n % 2][:, :],
                                             op0=ALU.mult, op1=ALU.add).then_inc(ss_read, 1)

            def qk_refine(g):
                if QKV_KIND[g] != "v":
                    n = qk_count(g)
                    dve.wait_ge(root_ready, 3 * n + 3)
                    if n:
                        dve.wait_ge(pre_ready, n)
                    refine(fix, root, root_sq, mean_sq, fix_ready, 2 * n + 2)

            def qk_norm(g):
                if QKV_KIND[g] != "v":
                    n = qk_count(g)
                    dve.wait_ge(fix_ready, 2 * n + 2)
                    if n >= 2:
                        dve.wait_ge(qk_lo_ready, n - 1)
                    dve.wait_ge(par_ready, 2)
                    c = norm_column(g)
                    to = pre[n % 2][:, ::-1] if QKV_KIND[g] == "k" else pre[n % 2]
                    dve.scalar_tensor_tensor(out=to, in0=acc(g)[:, :], scalar=par[:, c:c + 1],
                                             in1=fix, op0=ALU.mult, op1=ALU.mult).then_inc(pre_ready, 1)

            def v_scale(g):
                if QKV_KIND[g] == "v":
                    n = v_count(g)
                    dve.wait_ge(slab_done, g + 1)
                    dve.wait_ge(r_ready, 2)
                    if n:
                        dve.wait_ge(v_lo_ready, n)
                    dve.tensor_tensor(pre_v[:, ::-1], acc(g)[:, :], r_all[:, :], ALU.mult).then_inc(pre_v_ready, 1)

            def v_split_lo(g):
                if QKV_KIND[g] == "v":
                    t = QKV_TILE[g]
                    dve.wait_ge(v_hi_ready, v_count(g) + 1)
                    dve.tensor_tensor(v_parts[:, t, :, 1::2, :],
                                      bank[5][:, :].rearrange("p (t e d) -> p t e d", t=QT, e=2),
                                      v_parts[:, t, :, 0::2, :].bitcast(F32),
                                      ALU.subtract).then_inc(v_lo_ready, 1)

            def k_twice(t):
                dve.wait_ge(qk_hi_ready, qk_count(K_SLAB[t]) + 1)
                dve.tensor_copy(even[ODD, t, :], even[EVEN, t, :].bitcast(F32))
                dve.tensor_copy(odd[EVEN, t, :], odd[ODD, t, :].bitcast(F32)).then_inc(k_twice_ready, 1)

            for g in range(N_QKV):
                if g >= N_QKV - 4:
                    k_twice(5 + g - (N_QKV - 4))
                if g == N_QKV - 1:
                    k_twice(0)
                if g and QKV_KIND[g - 1] == "v":
                    v_split_lo(g - 1)
                v_scale(g)
                early = g <= 4 or g == 7
                if not early:
                    qk_refine(g - 1)
                qk_split_squares(g)
                if g and early:
                    qk_refine(g - 1)
                if g:
                    qk_norm(g - 1)
                qk_mean(g)
                if g == V_B - 1:
                    dve.wait_ge(r_root_ready, 3)
                    refine(r_all[:, :], r_root, r_root_sq, r_inv_sq, r_ready, 2)
                if g == 9:
                    dve.wait_ge(tab_done, 1)
                    dve.tensor_copy(tab[:, 0:S], bank[7][0:NH, :]).then_inc(tab_copied, 1)
                    dve.tensor_copy(tab[:, S:N_TAB], bank[6][0:NH, :]).then_inc(tab_copied, 1)

            def scores_max(i, half):
                for qt in HALVES[half]:
                    n = order(i, qt)
                    k0, nk = key_tiles(i, qt)
                    dve.wait_ge(scores_done, n + 1)
                    if qt == 3:
                        dve.wait_ge(bias_arrived[i % 2], 16 * (i // 2 + 1))
                    dve.tensor_tensor_reduce(
                        out=probs[:, P_BASE[qt]:P_BASE[qt] + P * nk], in0=bank[2 + (n + 1) % 3][:, 0:P * nk],
                        in1=bias_m[:, i % 2, 0:P * nk], scale=1.0, scalar=-3e38,
                        op0=ALU.add, op1=ALU.max, accum_out=top[:, qt:qt + 1]).then_inc(max_ready, 1)
                a = HALVES[half][1]
                dve.wait_ge(max_ready, QT * i + 2 * half + 2)
                if i < 8:
                    dve.tensor_scalar(neg[:, a:a + 2], top[:, a:a + 2], par[:, C_SINK + i:C_SINK + i + 1],
                                      -1.0, ALU.max, ALU.mult).then_inc(neg_ready, 1)
                else:
                    dve.tensor_scalar(neg[:, a:a + 2], top[:, a:a + 2], -1.0, None,
                                      ALU.mult).then_inc(neg_ready, 1)

            def normalise(i, half):
                a = HALVES[half][1]
                dve.wait_ge(exp_ready, QT * i + 2 * half + 2)
                if i < 8:
                    dve.wait_ge(sink_ready, 2 * i + half + 1)
                    dve.tensor_tensor(den[:, a:a + 2], den[:, a:a + 2], sink_e[:, a:a + 2],
                                      ALU.add).then_inc(den_ready, 1)
                    dve.wait_ge(den_ready, 2 * i + half + 1)
                dve.reciprocal(rec[:, a:a + 2], den[:, a:a + 2]).then_inc(rec_ready, 1)
                dve.wait_ge(rec_ready, 2 * i + half + 1)
                for qt in HALVES[half]:
                    s = probs[:, P_BASE[qt]:P_BASE[qt] + P * key_tiles(i, qt)[1]]
                    dve.tensor_scalar(s, s, rec[:, qt:qt + 1], None, ALU.mult).then_inc(probs_ready, 1)

            def probs_t_lo(i, qt):
                n = order(i, qt)
                k0, nk = key_tiles(i, qt)
                dve.wait_ge(pt_hi_ready, n + 1)
                dve.tensor_tensor(pt_lo[:, k0:k0 + nk, P * qt:P * qt + P],
                                  bank[6 - n % 2][:, 0:P * nk].rearrange("p (k q) -> p k q", k=nk),
                                  pt_hi[:, k0:k0 + nk, P * qt:P * qt + P].bitcast(F32),
                                  ALU.subtract).then_inc(pt_lo_ready, 1)

            def gate_scale(j):
                dve.wait_ge(slab_done, G_GATE + j + 1)
                dve.tensor_tensor(store[:, j, :], bank[j % 2][:, :], r_all[:, :],
                                  ALU.mult).then_inc(acc_read, 1)

            def y_sum(i):
                dve.wait_ge(y_part_ready, i + 1)
                if i > 1 and i % 2 == 0:
                    dve.wait_ge(y_lo_ready, i // 2)
                dve.tensor_tensor(y_both[y_rows(i), :], bank[7][0:HD, :], y_part(i), ALU.add).then_inc(y_sum_ready, 1)

            def y_lo(i):
                t = y_tile(i)
                dve.wait_ge(y_hi_ready, i // 2 + 1)
                dve.tensor_tensor(qk_lo[:, t, :], y_both[:, :], qk_hi[:, t, :].bitcast(F32),
                                  ALU.subtract).then_inc(y_lo_ready, 1)

            scores_max(0, 0)
            normalise(0, 0)
            v_split_lo(N_QKV - 1)
            scores_max(0, 1)
            normalise(0, 1)
            for i in range(NH):
                probs_t_lo(i, 3)
                probs_t_lo(i, 2)
                if i + 1 < NH:
                    scores_max(i + 1, 0)
                if i < NH - 1:
                    gate_scale(i)
                    if i > 1 and i % 2:
                        y_lo(i - 2)
                if i:
                    y_sum(i - 1)
                probs_t_lo(i, 1)
                probs_t_lo(i, 0)
                if i + 1 < NH:
                    normalise(i + 1, 0)
                    scores_max(i + 1, 1)
                    normalise(i + 1, 1)
                if i == NH - 2:
                    y_lo(i - 1)
            gate_scale(NH - 1)
            y_sum(NH - 1)
            y_lo(NH - 1)

            for n in range(N_BRANCH):
                g = G_BRANCH + n
                dve.wait_ge(slab_done, g + 1)
                dve.wait_ge(gate_ready, 2 * n + 2)
                if n:
                    dve.wait_ge(m_lo_ready, n)
                dve.tensor_tensor(tmp_a, branch_banks(n)[1][:, :], store[:, n, :],
                                  ALU.mult).then_inc(part_ready, 1)
                dve.tensor_tensor(tmp_b, branch_banks(n)[0][:, :], store[:, 8 + n, :],
                                  ALU.mult).then_inc(acc_read, 1)
                if g + 2 == LATE:
                    dve.wait_ge(w_hi_ready, LATE + 3)
                    dve.wait_ge(w_lo_ready, LATE - 1)
                    dve.tensor_tensor(w_lo[:, LATE % WS, :], w_raw[:, LATE % RAW, :],
                                      w_hi[:, LATE % WS, :].bitcast(F32), ALU.subtract).then_inc(w_lo_ready, 1)
                dve.wait_ge(part_ready, n + 1)
                dve.wait_ge(acc_read, read(g))
                dve.tensor_tensor(tmp_a, tmp_a, tmp_b, ALU.add).then_inc(m_ready, 1)
                dve.wait_ge(m_hi_ready, n + 1)
                dve.tensor_tensor(x_lo[:, n, :], tmp_a, x_hi[:, n, :].bitcast(F32),
                                  ALU.subtract).then_inc(m_lo_ready, 1)

            for n in range(N_OUT):
                g = G_OUT + n
                dve.wait_ge(slab_done, g + 1)
                dve.wait_ge(x2_arrived[n], 16)
                dve.tensor_tensor(store[:, n, :], bank[4 + n % 2][:, :], store[:, n, :],
                                  ALU.add).then_inc(acc_read, 1)
                dve.memset(store[:, 8 + n, :], 0.0)
                dve.wait_ge(x1_hi_ready, n + 1)
                dve.scalar_tensor_tensor(out=qk_lo[:, n, :], in0=store[:, n, :],
                                         scalar=par[:, C_FFN + n:C_FFN + n + 1],
                                         in1=qk_hi[:, n, :].bitcast(F32), op0=ALU.mult,
                                         op1=ALU.subtract).then_inc(x1_lo_ready, 1)
                if n:
                    dve.wait_ge(x1sq_ready, n + 1)
                    if n > 1:
                        dve.wait_ge(x1sum_ready, n - 1)
                    dve.tensor_tensor(r_all[:, :], r_all[:, :], (tmp_a, tmp_b)[n % 2],
                                      ALU.add).then_inc(x1sum_ready, 1)

            def up(j, c):
                g = G_FF + j
                dve.wait_ge(relu_ready, c * 8 + (j + 1))
                if j:
                    dve.wait_ge(u_lo_ready, c * 8 + j)
                dve.tensor_tensor(tmp_b, tmp_a, tmp_a, ALU.mult).then_inc(acc_read, 1)
                dve.wait_ge(u_hi_ready, c * 8 + (j + 1))
                dve.tensor_tensor(x_lo[:, j, :], tmp_b, x_hi[:, j, :].bitcast(F32),
                                  ALU.subtract).then_inc(u_lo_ready, 1)

            with dve.Fori(0, CHUNKS - 1) as c:
                for j in range(8):
                    up(j, c)
                for n in range(8):
                    g = G_FF + 8 + n
                    dve.wait_ge(slab_done, c * PER_CHUNK + (g + 1))
                    dve.tensor_tensor(store[:, 8 + n, :], bank[g % 2][:, :], store[:, 8 + n, :],
                                      ALU.add).then_inc(acc_read, 1)
            dve.wait_ge(ms2_done, 1)
            dve.tensor_scalar(r_all[:, :], bank[6][:, :], EPS, None, ALU.add).then_inc(ms2_ready, 1)
            dve.wait_ge(ms2_ready, 1)
            dve.reciprocal(r_all[:, :], r_all[:, :]).then_inc(r2_ready, 1)
            for j in range(8):
                up(j, CHUNKS - 1)
            for n in range(8):
                g = N_SLABS - 8 + n
                o = store[:, 8 + n, :]
                dve.wait_ge(r2_ready, 1)
                dve.tensor_tensor(o, o, r_all[:, :], ALU.mult).then_inc(scaled_ready, 1)
                dve.wait_ge(scaled_ready, n + 1)
                dve.tensor_tensor(o, o, store[:, n, :], ALU.add).then_inc(rest_sum_ready, 1)
                dve.wait_ge(rest_sum_ready, n + 1)
                for h, part in enumerate(HALF_TOKENS if n == 7 else [slice(0, S)]):
                    if n < 7 or h:
                        dve.wait_ge(slab_done, g + 1)
                    else:
                        dve.wait_ge(half_done, 1)
                    if n:
                        dve.wait_ge(out_ready, n)
                    dve.tensor_tensor(tmp_a[:, part], bank[2 if h else g % 2][:, part], r_all[:, part],
                                      ALU.mult).then_inc(acc_read, 1)
                    dve.wait_ge(acc_read, read(g) + h)
                    dve.tensor_tensor(o[:, part], tmp_a[:, part], o[:, part], ALU.add).then_inc(out_ready, 1)

        @block.tensor
        def _(pe):
            def products(out_, pairs, start, stop):
                last = None
                for a, (wh, wl, xh, xl) in enumerate(pairs):
                    first, end = start and a == 0, stop and a == len(pairs) - 1
                    pe.matmul(out_, wh, xh, start=first, stop=False)
                    pe.matmul(out_, wh, xl, start=False, stop=False)
                    last = pe.matmul(out_, wl, xh, start=False, stop=end)
                return last

            def weight(g, kt):
                c = slice(P * kt, P * kt + P)
                return w_hi[:, g % WS, c], w_lo[:, g % WS, c]

            def slab_part(g, acc, moving, kts, start=True, stop=True):
                return products(acc[:, :], [weight(g, kt) + moving(kt) for kt in kts], start, stop)

            def from_x(kt):
                return x_hi[:, kt, :], x_lo[:, kt, :]

            def from_qk(kt):
                return qk_hi[:, kt, :], qk_lo[:, kt, :]

            def head_norm_sum(g):
                n = qk_count(g)
                pe.wait_ge(sq_lo_ready, n + 1)
                if n >= 2:
                    pe.wait_ge(ss_read, n - 1)
                o = bank[3 + n % 2][:, :]
                pe.matmul(o, head_ones, sq_hi, start=True, stop=False)
                pe.matmul(o, head_ones, sq_lo, start=False, stop=True).then_inc(ss_done, 1)

            def v_transpose(g):
                pe.wait_ge(pre_v_ready, v_count(g) + 1)
                if v_count(g):
                    pe.wait_ge(v_lo_ready, v_count(g))
                for t in range(QT):
                    last = pe.transpose(bank[5][:, P * t:P * t + P], pre_v[:, P * t:P * t + P], ident[:, :])
                last.then_inc(vt_done, 1)

            def after(g):
                if QKV_KIND[g] == "v":
                    v_transpose(g)
                else:
                    head_norm_sum(g)

            def qkv_read(g):
                if QKV_KIND[g] == "v":
                    pe.wait_ge(pre_v_ready, v_count(g) + 1)
                else:
                    pe.wait_ge(pre_ready, qk_count(g) + 1)

            def mean_square(total, out_):
                return pe.matmul(out_[:, :], ones[:, :].to_broadcast([P, P]), total, start=True, stop=True)

            pe.wait_ge(const_ready, 1)
            for _ in range(WARM_UP):
                pe.matmul(bank[7][:, 0:P], ones[:, :].to_broadcast([P, P]), ones[:, :].to_broadcast([P, P]), start=True, stop=True)
            pe.wait_ge(const_ready, 3)
            pe.wait_ge(ident_ready, 2)
            AFTER = {2: 7, 3: 6, 4: 5, 5: 6, 6: 7, 7: 7, 8: 5, 9: 4, 10: 4, 11: 4, 12: 4, 13: 4, 14: 4}
            for g in range(N_QKV):
                if g > 1:
                    pe.wait_ge(w_lo_ready, g)
                if g > 8:
                    qkv_read(g - 3)
                elif g > 5:
                    qkv_read(g - 6)
                if g == 4:
                    pe.wait_ge(ms_ready, 1)
                for kt in range(KT):
                    if g < 2:
                        if kt < FIRST:
                            pe.wait_ge(first_ready, g + 1)
                        elif g and kt >= KT - FIRST:
                            pe.wait_ge(w_lo_ready, 1)
                        else:
                            pe.wait_ge(rest_ready, N_REST * g + kt // FIRST)
                    if g == 0:
                        pe.wait_ge(x_lo_ready, kt + 1)
                    last = slab_part(g, acc(g), from_x, [kt], kt == 0, kt == KT - 1)
                    if g == 2 and kt == 2:
                        pe.wait_ge(xsum_ready, KT - 1)
                        mean_square(x_sum, bank[6]).then_inc(ms_done, 1)
                        after(0)
                    if g == 8 and kt == 6:
                        pe.wait_ge(tab_arrived, 32)
                        qkv_read(4)
                        qkv_read(5)
                        pe.matmul(bank[7][0:NH, :], tabw, hot[:, 0:S], start=True, stop=True)
                        pe.matmul(bank[6][0:NH, :], tabw, hot[:, S:N_TAB], start=True,
                                  stop=True).then_inc(tab_done, 1)
                    if g == V_B + 1 and kt == 5:
                        qkv_read(3)
                    if g >= 2 and kt == AFTER.get(g, 3 if QKV_KIND[g - 1] != "v" else 5):
                        after(g - 1)
                last.then_inc(slab_done, 1)

            def scores(i, qt):
                n = order(i, qt)
                own, parts = (ODD, odd) if i % 2 else (EVEN, even)
                q = (1 + i // 2) if i < 8 else (Y_A + i // 2 - 4)
                k = 0 if i < 8 else 5 + i // 2 - 4
                k0, nk = key_tiles(i, qt)
                qs, ks = slice(P * qt, P * qt + P), slice(P * k0, P * (k0 + nk))
                if n >= 3:
                    pe.wait_ge(max_ready, n - 2)
                o = bank[2 + (n + 1) % 3][:, 0:P * nk]
                pe.matmul(o, parts[:, q, qs], parts[:, k, ks], start=True, stop=False)
                pe.matmul(o, parts[own, q, qs], k_lo[own, k_tile(k), ks], start=False,
                          stop=True).then_inc(scores_done, 1)

            def probs_transpose(i, qt):
                n = order(i, qt)
                pe.wait_ge(probs_ready, n + 1)
                if n >= 2:
                    pe.wait_ge(pt_lo_ready, n - 1)
                for j in range(key_tiles(i, qt)[1]):
                    at = P_BASE[qt] + P * j
                    last = pe.transpose(bank[6 - n % 2][:, P * j:P * j + P], probs[:, at:at + P], ident[:, :])
                last.then_inc(pt_done, 1)

            def values(i):
                pe.wait_ge(pt_lo_ready, QT * (i + 1))
                if i:
                    pe.wait_ge(y_sum_ready, i)
                v = 0 if i < 8 else 1 + i // 2 - 4
                e = i % 2
                for kt in reversed(range(QT)):
                    q0 = P * (QT - 1 - kt)
                    q1 = min(S, q0 + 2 * P) if i < 8 else S
                    both = v_parts[:, v, kt, 2 * e:2 * e + 2, :].rearrange("p a d -> p (a d)")
                    pe.matmul(bank[7][:, q0:q1], both, pt_hi[:, kt, q0:q1], start=(kt == QT - 1), stop=False,
                              skip_group_check=True)
                    last = pe.matmul(bank[7][0:HD, q0:q1], v_parts[:, v, kt, 2 * e, :],
                                     pt_lo[:, kt, q0:q1], start=False, stop=(kt == 0), skip_group_check=True)
                last.then_inc(pv_done, 1)

            def gate_part(j, kts, stop):
                g = G_GATE + j
                if kts[0] == 0:
                    pe.wait_ge(w_lo_ready, g)
                    if j < 2:
                        qkv_read(g - 3)
                    else:
                        pe.wait_ge(acc_read, read(g - 2))
                last = slab_part(g, bank[j % 2], from_x, kts, kts[0] == 0, stop)
                if stop:
                    last.then_inc(slab_done, 1)

            pe.wait_ge(qk_lo_ready, N_QK)
            pe.wait_ge(k_twice_ready, 5)
            scores(0, 3)
            scores(0, 2)
            gate_part(0, [0, 1, 2], False)
            pe.wait_ge(pre_v_ready, N_V)
            scores(0, 1)
            scores(0, 0)
            after(N_QKV - 1)
            gate_part(0, [3, 4, 5, 6, 7], True)
            for i in range(NH - 1):
                probs_transpose(i, 3)
                if i == 0:
                    pe.wait_ge(v_lo_ready, N_V)
                probs_transpose(i, 2)
                scores(i + 1, 3)
                scores(i + 1, 2)
                gate_part(i + 1, [0, 1, 2], False)
                probs_transpose(i, 1)
                probs_transpose(i, 0)
                scores(i + 1, 1)
                scores(i + 1, 0)
                gate_part(i + 1, [3, 4, 5, 6, 7], True)
                values(i)

            def branch_b(n, kts=(0, 1, 2, 3)):
                g = G_BRANCH + n
                if kts[0] == 0:
                    pe.wait_ge(w_lo_ready, g)
                    if n == 0:
                        pe.wait_ge(acc_read, read(g - 2))
                    elif n == 1:
                        pe.wait_ge(max_ready, QT * NH)
                    else:
                        pe.wait_ge(acc_read, read(g - 2))
                slab_part(g, branch_banks(n)[0], lambda kt: from_qk(Y_B + kt), kts, kts[0] == 0, kts[-1] == 3)

            def branch_a(n, kts):
                last = slab_part(G_BRANCH + n, branch_banks(n)[1], lambda kt: from_qk(Y_A + kt - 4), kts,
                                 kts[0] == 4, kts[-1] == 7)
                if kts[-1] == 7:
                    last.then_inc(slab_done, 1)

            probs_transpose(NH - 1, 3)
            probs_transpose(NH - 1, 2)
            branch_b(0)
            probs_transpose(NH - 1, 1)
            probs_transpose(NH - 1, 0)
            pe.wait_ge(max_ready, QT * NH)
            pe.wait_ge(y_lo_ready, NH // 2 - 2)
            branch_a(0, [4, 5])
            values(NH - 1)
            pe.wait_ge(y_lo_ready, NH // 2 - 1)
            branch_a(0, [6])
            branch_b(1)
            pe.wait_ge(y_lo_ready, NH // 2)
            branch_a(0, [7])
            pe.wait_ge(acc_read, read(G_BRANCH - 1))
            branch_a(1, [4, 5, 6, 7])
            for n in range(2, N_BRANCH):
                branch_b(n)
                branch_a(n, [4, 5, 6, 7])

            for n in range(N_OUT):
                g = G_OUT + n
                pe.wait_ge(w_lo_ready, g)
                if n >= 2:
                    pe.wait_ge(acc_read, read(g - 2))
                for kt in range(KT):
                    if n == 0:
                        pe.wait_ge(m_lo_ready, kt + 1)
                    last = slab_part(g, bank[4 + n % 2], from_x, [kt], kt == 0, kt == KT - 1)
                last.then_inc(slab_done, 1)

            def feed_forward(c, last_chunk=False):
                at = c * PER_CHUNK
                for j in range(8):
                    g = G_FF + j
                    pe.wait_ge(w_lo_ready, at + g)
                    pe.wait_ge(acc_read, at + read(g - 2))
                    for kt in range(KT):
                        if j == 0:
                            pe.wait_ge(x1_lo_ready, kt + 1)
                        last = slab_part(g, bank[g % 2], from_qk, [kt], kt == 0, kt == KT - 1)
                    last.then_inc(slab_done, 1)
                for n in range(8):
                    g = G_FF + 8 + n
                    pe.wait_ge(w_lo_ready, at + g)
                    pe.wait_ge(acc_read, at + read(g - 2))
                    if last_chunk and n == 7:
                        for part, b, done in zip(HALF_TOKENS, (g % 2, 2), (half_done, slab_done)):
                            last = products(bank[b][:, part], [weight(g, kt) + tuple(a[:, part] for a in from_x(kt))
                                                                   for kt in range(KT)], True, True)
                            last.then_inc(done, 1)
                        break
                    for kt in range(KT):
                        if n == 0:
                            pe.wait_ge(u_lo_ready, c * 8 + (kt + 1))
                        last = slab_part(g, bank[g % 2], from_x, [kt], kt == 0, kt == KT - 1)
                    last.then_inc(slab_done, 1)

            with pe.Fori(0, CHUNKS - 1) as c:
                feed_forward(c)
            pe.wait_ge(x1sum_ready, N_OUT - 1)
            mean_square(r_all[:, :], bank[6]).then_inc(ms2_done, 1)
            feed_forward(CHUNKS - 1, True)


def rel_bucket(n):
    n = np.maximum(n, 0)
    exact = NBUCKET // 2
    nf = np.maximum(n, 1).astype(np.float32)
    large = exact + (np.log(nf / np.float32(exact)) / np.float32(np.log(MAXDIST / exact))
                     * np.float32(NBUCKET - exact)).astype(np.int32)
    return np.where(n < exact, n, np.minimum(large, NBUCKET - 1))


def distance_onehot():
    hot = np.zeros((NBUCKET + 1, N_TAB), np.float32)
    for at, n, limit in ((T_A, T_B, S), (T_B, N_TAB - T_B, WINDOW)):
        d = np.arange(n) - (P - 1)
        row = np.where((d >= 0) & (d < limit), rel_bucket(d), NBUCKET)
        hot[row, at + np.arange(n)] = 1.0
    return hot


def as_slabs(w):
    n = w.shape[1] // P
    return w.reshape(KT, P, n, P).transpose(2, 1, 0, 3).reshape(n, P, D)


def kernel(**inputs):
    import concourse.bacc as bacc
    from concourse.bass_utils import run_bass_kernel_spmd

    a = {k: np.asarray(v) for k, v in inputs.items()}
    order_b = [t + 4 * e for t in range(4) for e in range(2)]
    w_in = a["w_in"][0]
    wa = 8 * HD
    at = np.cumsum([0, wa, wa, wa, wa, 2 * HD, 2 * HD, D])
    qa, ka, va, qb, kb, vb, ga, gb = (w_in[:, i:j] for i, j in zip(at, [*at[1:], w_in.shape[1]]))
    qb = qb.reshape(D, 8, HD)[:, order_b].reshape(D, wa)
    ka, qa = ka.reshape(D, 4, P), qa.reshape(D, 4, P)
    kq = [t[:, p] for p in range(4) for t in (ka, qa)]
    w_qkv = np.concatenate([kb, qb, vb, *kq, va, ga, gb], axis=1)
    branch_b = a["w_branch_b"][0].reshape(8, HD, D)[order_b].reshape(wa, D)
    w_branch = np.concatenate([branch_b, a["w_branch_a"][0]], axis=0)
    ff1 = as_slabs(a["w_ff1"][0]).reshape(CHUNKS, 8, P, D)
    ff2 = np.stack([as_slabs(w) for w in a["w_ff2"][0].reshape(CHUNKS, D, D)])
    slabs = np.concatenate([as_slabs(w_qkv), as_slabs(w_branch), as_slabs(a["w_out"][0]),
                            np.concatenate([ff1, ff2], axis=1).reshape(CHUNKS * PER_CHUNK, P, D)])

    def columns(v):
        return v.reshape(-1, P).T

    def twice(v):
        return np.tile(v.reshape(-1, 1), (2, 1))

    params = np.concatenate(
        [columns(a["g_mix"]), columns(a["g_ffn"]), columns(a["b_gate"]), twice(a["k_norm_b"]),
         twice(a["q_norm_b"]), twice(a["k_norm_a"]), twice(a["q_norm_a"]),
         np.tile(a["sinks"].reshape(1, 8)[:, order_b], (P, 1))], axis=1)
    table = np.concatenate([a["rel_bias"][:, 8:][:, order_b], a["rel_bias"][:, :8]], axis=1)
    arrays = {
        "x_t": a["x"].reshape(S, D).T.reshape(KT, P, S),
        "slabs": slabs, "params": params, "table": table, "onehot": distance_onehot(),
    }
    arrays = {k: np.ascontiguousarray(v) for k, v in arrays.items()}
    nc = bacc.Bacc("TRN2", target_bir_lowering=False, num_devices=1)
    F32 = mybir.dt.float32
    aps = [nc.dram_tensor(k, v.shape, F32, kind="ExternalInput").ap() for k, v in arrays.items()]
    tab_dram = nc.dram_tensor("tab_dram", (NH, N_TAB), F32, kind="Internal").ap()
    out = nc.dram_tensor("out", (KT, P, S), F32, kind="ExternalOutput").ap()
    build(nc, *aps, tab_dram, out)
    r = run_bass_kernel_spmd(nc, [arrays], core_ids=[0])
    return r.results[0]["out"].reshape(D, S).T.reshape(1, S, D)
```
